# Optimizing a Trainium2 kernel written in Bass

```python
import math
import jax
import jax.numpy as jnp
from jax import lax
import numpy as np

D_MODEL = 1024
BATCH = 1
SEQ = 256
DEPTH = 2

HEAD_DIM = 64
HEADS_PER_GROUP = 8
DILATED_GROUPS = ((128, 1), (512, 4), (2048, 16))
N_ATTN_GROUPS = len(DILATED_GROUPS)
ATTN_WIDTH = N_ATTN_GROUPS * HEADS_PER_GROUP * HEAD_DIM
ATTN_OUT_WIDTH = HEADS_PER_GROUP * HEAD_DIM
QUERY_BLOCK = 128
ROPE_THETA = 10000.0
LRU_WIDTH = D_MODEL
LRU_BLOCKS = 16
LRU_BLOCK_WIDTH = LRU_WIDTH // LRU_BLOCKS
CONV_WIDTH = 4
LRU_C = 8.0
N_BRANCHES = 2
N_IN = 3 * ATTN_WIDTH + 2 * LRU_WIDTH + N_BRANCHES * D_MODEL
N_GROUPS = 4
EXPERTS_PER_GROUP = 4
N_EXPERTS = N_GROUPS * EXPERTS_PER_GROUP
TOP_K_IN_GROUP = 2
D_EXPERT = 512
EPS = 1e-6

kernel_name = "hybrid_dilated_attn_rglru_hmoe"

def rmsnorm(x, scale):
    x32 = x.astype(jnp.float32)
    y = x32 * lax.rsqrt(jnp.mean(x32 * x32, axis=-1, keepdims=True) + EPS)
    return (y * scale.astype(jnp.float32)).astype(x.dtype)

def rotary_tables(seq_len):
    inv = ROPE_THETA ** (-jnp.arange(0, HEAD_DIM, 2, dtype=jnp.float32) / HEAD_DIM)
    ang = jnp.arange(seq_len, dtype=jnp.float32)[:, None] * inv[None, :]
    return jnp.cos(ang), jnp.sin(ang)

def apply_rope(x, cos, sin):
    half = x.shape[-1] // 2
    x32 = x.astype(jnp.float32)
    x1, x2 = x32[..., :half], x32[..., half:]
    c, s = cos[None, :, None, :], sin[None, :, None, :]
    return jnp.concatenate([x1 * c - x2 * s, x2 * c + x1 * s], axis=-1).astype(x.dtype)

def dilated_window_attention(q, k, v, window, dilation):
    B, S, H, E = q.shape
    L = S // dilation
    W = window // dilation
    Q = math.gcd(L, QUERY_BLOCK)
    nblk = L // Q
    qb = q.reshape(B, nblk, Q, dilation, H, E)
    pad = ((0, 0), (W, 0), (0, 0), (0, 0), (0, 0))
    kp = jnp.pad(k.reshape(B, L, dilation, H, E), pad)
    vp = jnp.pad(v.reshape(B, L, dilation, H, E), pad)
    key_idx = jnp.arange(nblk)[:, None] * Q + jnp.arange(Q + W)[None, :]
    kb = kp[:, key_idx]
    vb = vp[:, key_idx]
    s = jnp.einsum('bnqrhe,bnkrhe->bnrhqk', qb, kb).astype(jnp.float32) * (HEAD_DIM ** -0.5)
    dist = jnp.arange(Q)[:, None] + W - jnp.arange(Q + W)[None, :]
    valid = (dist >= 0) & (dist <= W) & (key_idx[:, None, :] >= W)
    s = jnp.where(valid[None, :, None, None], s, -jnp.inf)
    mx = jnp.max(s, axis=-1, keepdims=True)
    p = jnp.exp(s - mx)
    den = jnp.sum(p, axis=-1, keepdims=True)
    o = jnp.einsum('bnrhqk,bnkrhe->bnqrhe', (p / den).astype(v.dtype), vb)
    lse = (mx + jnp.log(den))[..., 0]
    o = o.reshape(B, S, H, E)
    lse = jnp.transpose(lse, (0, 1, 4, 2, 3)).reshape(B, S, H)
    return o, lse

def rg_lru(x, wa, ba, wx, bx, lam):
    B, S, _ = x.shape
    xb = x.reshape(B, S, LRU_BLOCKS, LRU_BLOCK_WIDTH)
    r = jax.nn.sigmoid(jnp.einsum('bsni,nij->bsnj', xb, wa).reshape(B, S, LRU_WIDTH) + ba)
    i = jax.nn.sigmoid(jnp.einsum('bsni,nij->bsnj', xb, wx).reshape(B, S, LRU_WIDTH) + bx)
    log_a = -LRU_C * r.astype(jnp.float32) * jax.nn.softplus(-lam.astype(jnp.float32))
    a = jnp.exp(log_a)
    b = jnp.sqrt(-jnp.expm1(2.0 * log_a)) * (i * x).astype(jnp.float32)

    def combine(left, right):
        al, bl = left
        ar, br = right
        return al * ar, ar * bl + br

    _, h = lax.associative_scan(combine, (a, b), axis=1)
    return h.astype(x.dtype)

def moe_ffn(h, wg, bg, we, be, w_gate, w_up, w_down):
    B, S, D = h.shape
    xt = h.reshape(B * S, D)
    g_logits = (xt @ wg + bg).astype(jnp.float32)
    g_prob = jax.nn.softmax(g_logits, axis=-1)
    g_idx = jnp.argmax(g_logits, axis=-1)
    g_w = jnp.take_along_axis(g_prob, g_idx[:, None], axis=-1)
    e_logits = (xt @ we + be).astype(jnp.float32).reshape(-1, N_GROUPS, EXPERTS_PER_GROUP)
    e_sel = jnp.take_along_axis(e_logits, g_idx[:, None, None], axis=1)[:, 0]
    top_v, top_i = lax.top_k(e_sel, TOP_K_IN_GROUP)
    w_top = jax.nn.softmax(top_v, axis=-1) * g_w
    expert_id = g_idx[:, None] * EXPERTS_PER_GROUP + top_i
    combine = jnp.sum(jax.nn.one_hot(expert_id, N_EXPERTS, dtype=jnp.float32) * w_top[..., None], axis=1)
    out = jnp.zeros((B * S, D), jnp.float32)
    for e in range(N_EXPERTS):
        act = jax.nn.silu(xt @ w_gate[e]) * (xt @ w_up[e])
        out = out + combine[:, e:e + 1] * (act @ w_down[e]).astype(jnp.float32)
    return out.reshape(B, S, D).astype(h.dtype)

def hybrid_layer(x, cos, sin, norm1, w_in, b_merge, conv_w, conv_b, lru_wa, lru_ba, lru_wx, lru_bx,
                 lru_lambda, w_proj_attn, w_proj_lru, w_out, norm2, router_group_w, router_group_b,
                 router_expert_w, router_expert_b, expert_w_gate, expert_w_up, expert_w_down):
    B, S, _ = x.shape
    h = rmsnorm(x, norm1)
    proj = h @ w_in
    cuts = [ATTN_WIDTH, 2 * ATTN_WIDTH, 3 * ATTN_WIDTH, 3 * ATTN_WIDTH + LRU_WIDTH, 3 * ATTN_WIDTH + 2 * LRU_WIDTH]
    q, k, v, u, g_lru, merge_logits = jnp.split(proj, cuts, axis=-1)
    n_heads = N_ATTN_GROUPS * HEADS_PER_GROUP
    q = apply_rope(q.reshape(B, S, n_heads, HEAD_DIM), cos, sin).reshape(B, S, N_ATTN_GROUPS, HEADS_PER_GROUP, HEAD_DIM)
    k = apply_rope(k.reshape(B, S, n_heads, HEAD_DIM), cos, sin).reshape(B, S, N_ATTN_GROUPS, HEADS_PER_GROUP, HEAD_DIM)
    v = v.reshape(B, S, N_ATTN_GROUPS, HEADS_PER_GROUP, HEAD_DIM)
    outs, lses = [], []
    for gi, (window, dilation) in enumerate(DILATED_GROUPS):
        o, lse = dilated_window_attention(q[:, :, gi], k[:, :, gi], v[:, :, gi], window, dilation)
        outs.append(o)
        lses.append(lse)
    alpha = jax.nn.softmax(jnp.stack(lses, axis=0), axis=0)
    attn = jnp.einsum('gbsh,gbshe->bshe', alpha, jnp.stack(outs, axis=0).astype(jnp.float32))
    attn = attn.reshape(B, S, ATTN_OUT_WIDTH).astype(x.dtype)
    u_pad = jnp.pad(u, ((0, 0), (CONV_WIDTH - 1, 0), (0, 0)))
    u_conv = sum(u_pad[:, j:j + S] * conv_w[j] for j in range(CONV_WIDTH)) + conv_b
    rec = rg_lru(u_conv, lru_wa, lru_ba, lru_wx, lru_bx, lru_lambda)
    lru_out = jax.nn.gelu(g_lru) * rec
    gates = jax.nn.sigmoid(merge_logits + b_merge).reshape(B, S, N_BRANCHES, D_MODEL)
    mixed = gates[:, :, 0] * (attn @ w_proj_attn) + gates[:, :, 1] * (lru_out @ w_proj_lru)
    x = x + mixed @ w_out
    h2 = rmsnorm(x, norm2)
    x = x + moe_ffn(h2, router_group_w, router_group_b, router_expert_w, router_expert_b,
                    expert_w_gate, expert_w_up, expert_w_down)
    return x

def setup_inputs(seed: int = 0) -> dict:
    key = jax.random.key(seed)
    ks = jax.random.split(key, 24)
    f32 = jnp.float32
    nrm = lambda k, shape, fan_in: jax.random.normal(k, shape, f32) * (fan_in ** -0.5)
    u = jax.random.uniform(ks[9], (DEPTH, LRU_WIDTH), f32, minval=0.9, maxval=0.999)
    a0 = u ** (1.0 / LRU_C)
    return {
        "x": jax.random.normal(ks[0], (BATCH, SEQ, D_MODEL), f32),
        "norm1_scale": 1.0 + 0.02 * jax.random.normal(ks[1], (DEPTH, D_MODEL), f32),
        "w_in": nrm(ks[2], (DEPTH, D_MODEL, N_IN), D_MODEL),
        "b_merge": 0.02 * jax.random.normal(ks[3], (DEPTH, N_BRANCHES * D_MODEL), f32),
        "conv_w": nrm(ks[4], (DEPTH, CONV_WIDTH, LRU_WIDTH), CONV_WIDTH),
        "conv_b": 0.02 * jax.random.normal(ks[5], (DEPTH, LRU_WIDTH), f32),
        "lru_wa": nrm(ks[6], (DEPTH, LRU_BLOCKS, LRU_BLOCK_WIDTH, LRU_BLOCK_WIDTH), LRU_BLOCK_WIDTH),
        "lru_ba": 0.02 * jax.random.normal(ks[7], (DEPTH, LRU_WIDTH), f32),
        "lru_wx": nrm(ks[8], (DEPTH, LRU_BLOCKS, LRU_BLOCK_WIDTH, LRU_BLOCK_WIDTH), LRU_BLOCK_WIDTH),
        "lru_bx": 0.02 * jax.random.normal(ks[10], (DEPTH, LRU_WIDTH), f32),
        "lru_lambda": jnp.log(a0) - jnp.log1p(-a0),
        "w_proj_attn": nrm(ks[11], (DEPTH, ATTN_OUT_WIDTH, D_MODEL), ATTN_OUT_WIDTH),
        "w_proj_lru": nrm(ks[12], (DEPTH, LRU_WIDTH, D_MODEL), LRU_WIDTH),
        "w_out": nrm(ks[13], (DEPTH, D_MODEL, D_MODEL), D_MODEL),
        "norm2_scale": 1.0 + 0.02 * jax.random.normal(ks[14], (DEPTH, D_MODEL), f32),
        "router_group_w": nrm(ks[15], (DEPTH, D_MODEL, N_GROUPS), D_MODEL),
        "router_group_b": 0.01 * jax.random.normal(ks[16], (DEPTH, N_GROUPS), f32),
        "router_expert_w": nrm(ks[17], (DEPTH, D_MODEL, N_EXPERTS), D_MODEL),
        "router_expert_b": 0.01 * jax.random.normal(ks[18], (DEPTH, N_EXPERTS), f32),
        "expert_w_gate": nrm(ks[19], (DEPTH, N_EXPERTS, D_MODEL, D_EXPERT), D_MODEL),
        "expert_w_up": nrm(ks[20], (DEPTH, N_EXPERTS, D_MODEL, D_EXPERT), D_MODEL),
        "expert_w_down": nrm(ks[21], (DEPTH, N_EXPERTS, D_EXPERT, D_MODEL), D_EXPERT),
        "final_norm_scale": 1.0 + 0.02 * jax.random.normal(ks[22], (D_MODEL,), f32),
    }

def reference(x, norm1_scale, w_in, b_merge, conv_w, conv_b, lru_wa, lru_ba, lru_wx, lru_bx,
              lru_lambda, w_proj_attn, w_proj_lru, w_out, norm2_scale, router_group_w, router_group_b,
              router_expert_w, router_expert_b, expert_w_gate, expert_w_up, expert_w_down,
              final_norm_scale):
    cos, sin = rotary_tables(x.shape[1])
    for l in range(DEPTH):
        x = hybrid_layer(x, cos, sin, norm1_scale[l], w_in[l], b_merge[l], conv_w[l], conv_b[l],
                         lru_wa[l], lru_ba[l], lru_wx[l], lru_bx[l], lru_lambda[l], w_proj_attn[l],
                         w_proj_lru[l], w_out[l], norm2_scale[l], router_group_w[l], router_group_b[l],
                         router_expert_w[l], router_expert_b[l], expert_w_gate[l], expert_w_up[l],
                         expert_w_down[l])
    return rmsnorm(x, final_norm_scale)


_drawn_inputs = setup_inputs


def setup_inputs(seed=0):
    import zlib

    import numpy as np

    out = dict(_drawn_inputs(seed))
    spreads = {}
    factors = {'b_merge': 6.326,
     'lru_ba': 23.562,
     'lru_bx': 8.0,
     'router_group_b': 3.221,
     'router_expert_b': 8.0,
     'final_norm_scale': 8.003}
    for name, (base, spread) in spreads.items():
        noise = np.random.default_rng([zlib.crc32(name.encode()), seed]).standard_normal(out[name].shape)
        drawn = base * np.exp(spread * noise) if base else spread * noise
        out[name] = jnp.asarray(drawn.astype(out[name].dtype))
    for name, factor in factors.items():
        out[name] = (out[name] * factor).astype(out[name].dtype)
    return out
```

```python
import math
from contextlib import ExitStack

import numpy as np

import concourse.bass as bass
from concourse import mybir

P = 128
D = 1024
S = 256
NT = S // P
KD = D // P
LAYERS = 2
GROUPS = 3
HEADS = 8
HD = 64
WINDOWS = ((128, 1), (512, 4), (2048, 16))
NE = 16
EG = 4
EPS = 1e-6
CAP = 64
MORE = S // CAP - 1
NEG = -1.0e30

UCOL = 4 * 512
W_UNITS = 44
E_UNITS = 6
M_UNITS = NE * E_UNITS
UNITS = W_UNITS + M_UNITS
SLOTS = 3
RAW = 6
RAW_SLOT = [u % SLOTS if u < W_UNITS else (u - W_UNITS) % RAW for u in range(UNITS)]
RAW_USES = [RAW_SLOT.count(s) for s in range(RAW)]
POOL_AT = 1280

GROUP_KINDS = (["u"] * 2 + ["q"] * 3 + ["k"] * 3 + ["v"] * 3 + ["g"] * 2 + ["m"] * 4 + ["pl"] * 2
               + ["pa"] * 2 + ["wo"] * 2)
GROUP_UNITS = [1 if kind == "pa" else 2 for kind in GROUP_KINDS]
GROUP_START = [sum(GROUP_UNITS[:i]) for i in range(len(GROUP_KINDS))]
GROUP_END = {GROUP_START[i] + GROUP_UNITS[i]: i for i in range(len(GROUP_KINDS))}
NG = len(GROUP_KINDS)
PAIR_READS = [len(range(b, NG - 2, 2)) for b in range(2)]
ATT0 = 11

C_N1, C_BA, C_BX, C_LAM, C_CB, C_CW, C_BM = 0, 8, 16, 24, 32, 40, 72
C_RW, C_RB, SMALL = 88, 248, 268


def turn(u):
    if u >= SLOTS:
        return u + 1
    last = max(v for v in range(UNITS) if v % SLOTS == u)
    return last - UNITS + 1 + SLOTS


def raw_turn(u):
    before = [v for v in range(u) if RAW_SLOT[v] == RAW_SLOT[u]]
    last = before[-1] if before else max(v for v in range(UNITS) if RAW_SLOT[v] == RAW_SLOT[u]) - UNITS
    return last + 1 + RAW


class Chain:

    def __init__(self, eng, sem):
        self.eng, self.sem, self.base, self.n = eng, sem, 0, 0

    def at(self, base):
        self.base, self.n = base, 0

    def link(self, ins):
        self.n += 1
        ins.then_inc(self.sem, 1)
        self.eng.wait_ge(self.sem, self.base + self.n)


DVE_LINKS = 128


def build(nc, stream, x, small, blockdiag, norm_rows, tables, masks, out):
    f32, f32r, bf16, i32, u32 = (mybir.dt.float32, mybir.dt.float32r, mybir.dt.bfloat16, mybir.dt.int32,
                                 mybir.dt.uint32)
    ALU, ACT, AX = mybir.AluOpType, mybir.ActivationFunctionType, mybir.AxisListType
    ds = bass.ds
    ctx = ExitStack()
    with ctx:
        def sb(name, shape, dt=f32):
            return ctx.enter_context(nc.sbuf_tensor(name, shape, dt))

        def sem(name):
            return ctx.enter_context(nc.semaphore(name))

        raws = sb("raws", [P, RAW, UCOL])
        raw = raws
        high = sb("high", [P, SLOTS, UCOL], f32r)
        low = sb("low", [P, SLOTS, UCOL], f32r)
        xs = sb("xs", [P, NT, D])
        act_h = sb("act_h", [P, 2048], f32r)
        act_l = sb("act_l", [P, 2048], f32r)
        lru_h = sb("lru_h", [P, 2048], f32r)
        lru_l = sb("lru_l", [P, 2048], f32r)
        att_h = sb("att_h", [P, 1024], f32r)
        att_l = sb("att_l", [P, 1024], f32r)
        qk = raws[:, SLOTS:RAW, :].rearrange("p s n -> p (s n)")
        qT = qk[:, 0:12 * S].rearrange("p (c n) -> p c n", c=12)
        kT = qk[:, 12 * S:24 * S].rearrange("p (c n) -> p c n", c=12)
        v = sb("v", [P, NT, GROUPS * 512])
        s0 = sb("s0", [P, 8 * 259])
        s1 = sb("s1", [P, 2048])
        s2 = sb("s2", [P, 2048])
        s3 = sb("s3", [P, 2048])
        at = sb("at", [P, 2176])
        mask = sb("mask", [P, GROUPS, S], bf16)
        ident, tri, ones = sb("ident", [P, P]), sb("tri", [P, P]), sb("ones", [P, P])
        iota = sb("iota", [P, 2 * CAP])
        cos2, sin2 = sb("cos2", [P, NT, HD]), sb("sin2", [P, NT, HD])
        smalls = sb("smalls", [P, LAYERS, SMALL])
        cur = sb("cur", [P, SMALL])
        sp = sb("sp", [P, 8, 8])
        ss, rstd, mhalf = sb("ss", [P, NT]), sb("rstd", [P, NT]), sb("mhalf", [P, NT])
        nmax, den, rden = sb("nmax", [P, NT]), sb("den", [P, NT]), sb("rden", [P, NT])
        lg = sb("lg", [P, NT, 20])
        g8, e8 = sb("g8", [P, NT, 8]), sb("e8", [P, NT, 8])
        gm, em = sb("gm", [P, NT, 8]), sb("em", [P, NT, 8])
        gi, ei = sb("gi", [P, NT, 8], u32), sb("ei", [P, NT, 8], u32)
        gf, ef = sb("gf", [P, NT, 8]), sb("ef", [P, NT, 8])
        goh, oh1, oh2 = sb("goh", [P, NT, EG]), sb("oh1", [P, NT, EG]), sb("oh2", [P, NT, EG])
        r16 = sb("r16", [P, NT, NE])
        rs = sb("rs", [P, 12, NT])
        sel, comb, rank = sb("sel", [P, NT, NE]), sb("comb", [P, NT, NE]), sb("rank", [P, NT, NE + 1])
        over = sb("over", [P, 1])
        flag = sb("flag", [P, 1], i32)
        ws = sb("ws", [P, 1])

        xn = s0[:, 0:2048].rearrange("p (t d) -> p t d", t=NT)
        junk = s3[:, :].rearrange("p (t d) -> p t d", t=NT)
        upad = s0[:, :].rearrange("p (c n) -> p c n", c=8)
        conv = s1[:, :].rearrange("p (c n) -> p c n", c=8)
        rg, ig = s2[:, :].rearrange("p (c n) -> p c n", c=8), s3[:, :].rearrange("p (c n) -> p c n", c=8)
        decay = s0[:, 0:2048].rearrange("p (c n) -> p c n", c=8)
        rec = s1
        probs = s3[:, 0:1152]
        bd = at[:, 0:2048].rearrange("p (w c n) -> p w c n", w=2, c=8)
        pT = at[:, 0:1152]
        attn = at[:, 1152:2176].rearrange("p (t n) -> p t n", t=NT)
        nrow = v[:, 0, 0:D]
        h2 = xn
        h2T = s2[:, :].rearrange("p (c n) -> p c n", c=8)
        g_low, u_low = s2[0:CAP, 0:512], s2[0:CAP, 512:1024]
        g_sum, tgate, u_sum, act = (s1[0:CAP, n * 512:(n + 1) * 512] for n in range(4))
        hT_h, hT_l = (a[:, :].rearrange("p (c n) -> p c n", c=8) for a in (act_h, act_l))
        h2_h, h2_l = (a[:, :].rearrange("p (t d) -> p t d", t=NT) for a in (act_h, act_l))
        lT_h, lT_l = (a[:, :].rearrange("p (c n) -> p c n", c=8) for a in (lru_h, lru_l))
        aT_h, aT_l = (a[:, :].rearrange("p (c n) -> p c n", c=4) for a in (att_h, att_l))
        he = lru_h[:, 0:1024].rearrange("p (c n) -> p c n", c=8)
        y_h, y_l = lru_h[:, 1024:2048], lru_l[:, 1024:2048]
        ae = att_h[:, 0:512].rearrange("p (c n) -> p c n", c=4)
        pe_01 = att_h[:, 512:768].rearrange("p (t n) -> p t n", t=NT)
        pt_01 = att_h[:, 768:1024]

        pair = [ctx.enter_context(nc.psum_tensor(f"pair{b}", [P, 1024], f32)) for b in range(2)]
        pS = ctx.enter_context(nc.psum_tensor("pS", [P, 1536], f32))
        pO = ctx.enter_context(nc.psum_tensor("pO", [P, 512], f32))
        bank = [pS[:, 0:512], pS[:, 512:1024], pS[:, 1024:1536], pO[:, :]]

        class Flow:

            def __init__(self, tag, units, first):
                self.units, self.first = units, first
                self.raw_uses = [(RAW_USES[s] if first else NE) for s in range(RAW)]
                self.raw_in = [sem(f"{tag}_raw_in{s}") for s in range(RAW)]
                self.high_ready = sem(f"{tag}_high_ready")
                self.low_dve = sem(f"{tag}_low_dve")
                self.low_pool = sem(f"{tag}_low_pool")
                self.unit_used = sem(f"{tag}_unit_used")
                self.p_ready = sem(f"{tag}_p_ready")
                self.pt_done = sem(f"{tag}_pt_done")
                self.pt_ready = sem(f"{tag}_pt_ready")
                self.ws_ready = sem(f"{tag}_ws_ready")
                self.he_done0 = sem(f"{tag}_he_done0")
                self.he_done1 = sem(f"{tag}_he_done1")
                self.he_high0 = sem(f"{tag}_he_high0")
                self.he_high1 = sem(f"{tag}_he_high1")
                self.he_low0 = sem(f"{tag}_he_low0")
                self.he_low1 = sem(f"{tag}_he_low1")
                self.g_low = sem(f"{tag}_g_low")
                self.g_sum = sem(f"{tag}_g_sum")
                self.u_low = sem(f"{tag}_u_low")
                self.u_sum = sem(f"{tag}_u_sum")
                self.tanh_ready = sem(f"{tag}_tanh_ready")
                self.act_ready = sem(f"{tag}_act_ready")
                self.aeT_done = sem(f"{tag}_aeT_done")
                self.ae_high = sem(f"{tag}_ae_high")
                self.ae_low = sem(f"{tag}_ae_low")
                self.y_high0 = sem(f"{tag}_y_high0")
                self.y_high1 = sem(f"{tag}_y_high1")
                self.y_low0 = sem(f"{tag}_y_low0")
                self.y_low1 = sem(f"{tag}_y_low1")
                self.y_zero = sem(f"{tag}_y_zero")
                self.moe_done = sem(f"{tag}_moe_done")
                self.x_added = sem(f"{tag}_x_added")
                self.dve_chain = sem(f"{tag}_dve_chain")

        main, over_flow = Flow("m", UNITS, W_UNITS), Flow("o", M_UNITS, 0)
        (const_in, x_in, bd_in, nrow_in, out_done) = (sem(n) for n in (
            "const_in", "x_in", "bd_in", "nrow_in", "out_done"))
        (ss_ready, rstd_ready, xn_ready, xT_done, hT_high, hT_low, pair_read0, pair_read1) = (sem(n) for n in (
             "ss_ready", "rstd_ready", "xn_ready", "xT_done", "hT_high", "hT_low", "pair_read0",
             "pair_read1"))
        pair_read = [pair_read0, pair_read1]
        (cur_ready, pad_zero, u_ready, conv_ready, gate_mm, r_ready, i_ready, sp_ready,
         elam_ready, decay_ready, t_ready, v_ready, root_ready, rec_ready) = (sem(n) for n in (
             "cur_ready", "pad_zero", "u_ready", "conv_ready", "gate_mm", "r_ready",
             "i_ready", "sp_ready", "elam_ready", "decay_ready", "t_ready", "v_ready", "root_ready",
             "rec_ready"))
        (rot_ready, rotT_done, qkT_ready, v_in, g_ready, g_inner, g_tanh, lru_full, lT_high, lT_low) = (sem(n) for n in (
             "rot_ready", "rotT_done", "qkT_ready", "v_in", "g_ready", "g_inner", "g_tanh", "lru_full",
             "lT_high", "lT_low"))
        (qk_done, max_ready, exp_ready, pT_done, pT_ready, pv_done, attn_ready, aT_done, aT_high, aT_low,
         mix_full, mix_high, mix_low, x_done) = (sem(n) for n in (
             "qk_done", "max_ready", "exp_ready", "pT_done", "pT_ready", "pv_done", "attn_ready", "aT_done",
             "aT_high", "aT_low", "mix_full", "mix_high", "mix_low", "x_done"))
        (h2_ready, h2_high, h2_low, h2T_done, h2T_ready, logits_done, gneg_ready, gexp_ready, diff_ready,
         e2_ready, sel_ready, rank_done, flag_ready, table_zero) = (sem(n) for n in (
             "h2_ready", "h2_high", "h2_low", "h2T_done", "h2T_ready", "logits_done", "gneg_ready",
             "gexp_ready", "diff_ready", "e2_ready", "sel_ready", "rank_done", "flag_ready", "table_zero"))
        dve_chain, pool_chain, mask_in, wait_carried, rank_moved = (sem(n) for n in (
            "dve_chain", "pool_chain", "mask_in", "wait_carried", "rank_moved"))

        block = ctx.enter_context(nc.Block())

        def settled(eng):
            eng.sem_inc(wait_carried, 1)

        @block.sync
        def _(sp_eng):
            eng = sp_eng
            eng.dma_start(xs[:, :, :], x).then_inc(x_in, 16)
            eng.dma_start(smalls[:, :, :], small).then_inc(const_in, 16)
            eng.dma_start(ident[:, :], tables[:, 0:128]).then_inc(const_in, 16)
            eng.dma_start(tri[:, :], tables[:, 128:256]).then_inc(const_in, 16)
            eng.dma_start(iota[:, :], tables[:, 256:384]).then_inc(const_in, 16)
            eng.dma_start(cos2[:, :, :], tables[:, 512:640].rearrange("p (t n) -> p t n", t=NT)
                          ).then_inc(const_in, 16)
            eng.dma_start(sin2[:, :, :], tables[:, 640:768].rearrange("p (t n) -> p t n", t=NT)
                          ).then_inc(const_in, 16)
            eng.dma_start(s2[:, 0:768], masks).then_inc(mask_in, 16)

            def load(flow, slot, after, unit_row):
                eng.wait_ge(flow.low_dve, after)
                eng.wait_ge(flow.low_pool, after)
                eng.dma_start(raw[:, slot, :], stream[ds(unit_row, 1), :, :].rearrange("o p n -> (o p) n")
                              ).then_inc(flow.raw_in[slot], 16)

            def load_expert(flow, l, e, first, row):
                for j in range(E_UNITS):
                    load(flow, j, l * flow.units + e * E_UNITS + (first + j + 1), row + j)

            with eng.Fori(0, LAYERS) as l:
                for u in range(W_UNITS + RAW):
                    if u == W_UNITS + SLOTS:
                        eng.wait_ge(qk_done, l * 8 + 8)
                    load(main, RAW_SLOT[u], l * UNITS + raw_turn(u), l * UNITS + u)
                with eng.Fori(1, NE) as e:
                    load_expert(main, l, e, W_UNITS, l * UNITS + e * E_UNITS + W_UNITS)
                eng.wait_ge(flag_ready, l + 1)
                settled(eng)
                more = eng.value_load(flag[0:1, 0:1], min_val=0, max_val=1)
                with eng.If(more > 0):
                    eng.wait_ge(main.low_dve, l * UNITS + UNITS + RAW)
                    eng.wait_ge(main.low_pool, l * UNITS + UNITS + RAW)
                    settled(eng)
                    with eng.Fori(0, MORE) as q:
                        with eng.Fori(0, NE) as e:
                            load_expert(over_flow, l * MORE + q, e, 0, l * UNITS + e * E_UNITS + W_UNITS)
                    eng.wait_ge(over_flow.low_dve, (l + 1) * (MORE * M_UNITS) + RAW)
                    eng.wait_ge(over_flow.low_pool, (l + 1) * (MORE * M_UNITS) + RAW)
                    settled(eng)
                with eng.Else():
                    for s in range(RAW):
                        eng.sem_inc(over_flow.raw_in[s], 16 * NE * MORE)
            for t in range(NT):
                eng.wait_ge(out_done, t + 1)
                eng.dma_start(out[:, t, :], xn[:, t, :]).then_inc(x_in, 16)
            eng.wait_ge(x_in, 16 * (1 + NT))

        @block.scalar
        def _(act_eng):
            eng = act_eng
            def split_high(flow, raw_slot, in_count, used_count, slot):
                eng.wait_ge(flow.raw_in[raw_slot], in_count)
                eng.wait_ge(flow.unit_used, used_count)
                nc.scalar.activation(high[:, slot, :], raw[:, raw_slot, :], ACT.Copy).then_inc(flow.high_ready, 1)

            def split_w(l, u):
                s = RAW_SLOT[u]
                split_high(main, s, (l * RAW_USES[s] + RAW_SLOT[:u + 1].count(s)) * 16, l * UNITS + turn(u),
                           u % SLOTS)

            def sum_squares():
                for t in range(NT):
                    nc.scalar.activation(junk[:, t, :], xs[:, t, :], ACT.Square,
                                         accum_out=ss[:, t:t + 1]).then_inc(ss_ready, 1)

            def load_row(row):
                eng.dma_start(nrow, norm_rows[ds(row, 1), :, :].rearrange("o p n -> (o p) n")
                              ).then_inc(nrow_in, 16)

            def moe(flow, l, first):
                def split(e, j):
                    before = flow.raw_uses[j] - NE
                    split_high(flow, j, (l * flow.raw_uses[j] + e + (before + 1)) * 16,
                               l * flow.units + e * E_UNITS + (first + j + 1), (first + j) % SLOTS)

                def evac_he(e_next, half):
                    eng.wait_ge([flow.he_done0, flow.he_done1][half], l * (NE + 1) + e_next + 1)
                    nc.scalar.activation(he[:, 4 * half:4 * half + 4, 0:CAP],
                                         bank[2 + half][:, 0:256].rearrange("p (c n) -> p c n", c=4), ACT.Copy
                                         ).then_inc([flow.he_high0, flow.he_high1][half], 1)

                def expert(e, last):
                    split(e, 2)
                    split(e, 3)
                    eng.wait_ge(flow.unit_used, l * flow.units + e * E_UNITS + (first + 2 + SLOTS))
                    nc.scalar.activation(g_low, bank[0][CAP:P, :], ACT.Copy).then_inc(flow.g_low, 1)
                    eng.wait_ge(flow.pt_done, l * NE + e + 1)
                    nc.scalar.activation(pt_01, bank[2][:, 0:S], ACT.Copy).then_inc(flow.pt_ready, 1)
                    eng.wait_ge(flow.g_sum, l * NE + e + 1)
                    nc.scalar.activation(tgate, g_sum, ACT.Tanh, scale=0.5).then_inc(flow.tanh_ready, 1)
                    split(e, 4)
                    eng.wait_ge(flow.unit_used, l * flow.units + e * E_UNITS + (first + 4 + SLOTS))
                    nc.scalar.activation(u_low, bank[1][CAP:P, :], ACT.Copy).then_inc(flow.u_low, 1)
                    split(e, 5)
                    evac_he(e + 1, 0)
                    eng.wait_ge(flow.aeT_done, l * NE + e + 1)
                    nc.scalar.activation(ae[:, :, 0:CAP], bank[0][:, 0:256].rearrange("p (c n) -> p c n", c=4),
                                         ACT.Copy
                                         ).then_inc(flow.ae_high, 1)
                    evac_he(e + 1, 1)
                    if not last:
                        split(e + 1, 0)
                    for half in range(2):
                        if half and not last:
                            split(e + 1, 1)
                        eng.wait_ge(flow.unit_used, l * flow.units + e * E_UNITS + (first + 5 + half + SLOTS))
                        eng.wait_ge(flow.ws_ready, l * NE + e + 1)
                        nc.scalar.activation(y_h[:, 512 * half:512 * half + 512], bank[1 + half], ACT.Copy,
                                             scale=ws[:, 0:1]).then_inc([flow.y_high0, flow.y_high1][half], 1)

                evac_he(0, 0)
                evac_he(0, 1)
                with eng.Fori(0, NE - 1) as e:
                    expert(e, False)
                expert(NE - 1, True)

            for flow in (main, over_flow):
                eng.sem_inc(flow.y_high0, 1)
                eng.sem_inc(flow.y_high1, 1)
            eng.wait_ge(x_in, 16)
            eng.wait_ge(const_in, 96)
            with eng.Fori(0, LAYERS) as l:
                eng.dma_start(at[:, 0:2048], blockdiag[ds(l, 1), :, :].rearrange("o p n -> (o p) n")
                              ).then_inc(bd_in, 16)
                eng.wait_ge(x_done, l + 1)
                sum_squares()
                eng.wait_ge(cur_ready, l * 2 + 2)
                for half in range(2):
                    split_w(l, half)
                    eng.wait_ge(xT_done, l * 2 + half + 1)
                    for c in range(4 * half, 4 * half + 4):
                        nc.scalar.activation(hT_h[:, c, :], pair[half][:, (c % 4) * S:(c % 4 + 1) * S], ACT.Copy,
                                             scale=cur[:, C_N1 + c:C_N1 + c + 1]).then_inc(hT_high, 1)
                eng.wait_ge(elam_ready, l * 2 + 1)
                nc.scalar.activation(sp[:, 2, :], sp[:, 1, :], ACT.Exp, scale=-1.0).then_inc(elam_ready, 1)

                for u in range(2, W_UNITS + 1):
                    split_w(l, u)
                    for p in ([u - 1] if u < W_UNITS else [W_UNITS - 1, W_UNITS]):
                        i = GROUP_END.get(p)
                        kind = GROUP_KINDS[i] if i is not None else None
                        b = None if i is None else i % 2
                        done = None if i is None else l * UNITS + (p + SLOTS)
                        if kind == "u":
                            c0 = 4 * i
                            eng.wait_ge(main.unit_used, done)
                            eng.wait_ge(pad_zero, l + 1)
                            nc.scalar.activation(upad[:, c0:c0 + 4, 3:3 + S],
                                                 pair[b][:, :].rearrange("p (c n) -> p c n", c=4), ACT.Copy
                                                 ).then_inc(u_ready, 1)
                            for c in range(4):
                                ins = nc.scalar.activation(conv[:, c0 + c, :], pair[b][:, c * S:(c + 1) * S],
                                                           ACT.Identity,
                                                           scale=cur[:, C_CW + 24 + c0 + c:C_CW + 25 + c0 + c],
                                                           bias=cur[:, C_CB + c0 + c:C_CB + c0 + c + 1])
                            ins.then_inc(pair_read[b], 1)
                        if kind == "v":
                            eng.wait_ge(main.unit_used, done)
                            g = i - 8
                            nc.scalar.activation(v[:, :, g * 512:(g + 1) * 512],
                                                 pair[b][:, :].rearrange("p (t n) -> p t n", t=NT), ACT.Copy
                                                 ).then_inc(pair_read[b], 1)
                        if 5 <= p <= 8:
                            for c in range(2 * (p - 5), 2 * (p - 5) + 2):
                                eng.wait_ge(gate_mm, l * 8 + c + 1)
                                ps = pS[:, (c % 3) * 512:(c % 3) * 512 + 512]
                                nc.scalar.activation(rg[:, c, :], ps[:, 0:S], ACT.Tanh, scale=0.5,
                                                     bias=cur[:, C_BA + c:C_BA + c + 1]).then_inc(r_ready, 1)
                                nc.scalar.activation(ig[:, c, :], ps[:, S:2 * S], ACT.Tanh, scale=0.5,
                                                     bias=cur[:, C_BX + c:C_BX + c + 1]).then_inc(i_ready, 1)
                        if p == 9:
                            eng.wait_ge(sp_ready, l * 2 + 2)
                            eng.wait_ge(conv_ready, l * 8 + 8)
                            eng.wait_ge(r_ready, l * 8 + 8)
                            for c in range(8):
                                nc.scalar.activation(decay[:, c, :], rg[:, c, :], ACT.Exp,
                                                     scale=sp[:, 6, c:c + 1], bias=sp[:, 6, c:c + 1]
                                                     ).then_inc(decay_ready, 1)
                                nc.scalar.activation(rg[:, c, :], rg[:, c, :], ACT.Tanh,
                                                     scale=sp[:, 7, c:c + 1], bias=sp[:, 7, c:c + 1]
                                                     ).then_inc(t_ready, 1)
                        if p == 12:
                            eng.wait_ge(v_ready, l + 1)
                            nc.scalar.activation(s2[:, :], s2[:, :], ACT.Sqrt, scale=0.25).then_inc(root_ready, 1)
                        for tile in range(NT):
                            j = GROUP_END.get(p - 1 - tile)
                            if j is not None and GROUP_KINDS[j] in "qk":
                                n = (j - 2) * NT + tile
                                eng.wait_ge(rotT_done, l * 12 + n + 1)
                                dst = qT if GROUP_KINDS[j] == "q" else kT
                                g = (j - 2) % 3
                                nc.scalar.activation(dst[:, 4 * g:4 * g + 4, tile * P:(tile + 1) * P],
                                                     pO[:, :].rearrange("p (c n) -> p c n", c=4), ACT.Copy
                                                     ).then_inc(qkT_ready, 1)
                        if kind == "g":
                            half = i - ATT0
                            eng.wait_ge(main.unit_used, done)
                            eng.wait_ge(rec_ready, l * 8 + 8)
                            nc.scalar.activation(s2[:, half * 1024:half * 1024 + 1024], pair[b][:, :], ACT.Square
                                                 ).then_inc(g_ready, 1)
                            nc.scalar.activation(s0[:, half * 1024:half * 1024 + 1024], pair[b][:, :], ACT.Copy
                                                 ).then_inc(pair_read[b], 1)
                            eng.wait_ge(g_inner, l * 2 + half + 1)
                            nc.scalar.activation(s2[:, half * 1024:half * 1024 + 1024],
                                                 s2[:, half * 1024:half * 1024 + 1024], ACT.Tanh,
                                                 scale=math.sqrt(2.0 / math.pi)).then_inc(g_tanh, 1)
                            eng.wait_ge(lru_full, l * 2 + half + 1)
                            nc.scalar.activation(lru_h[:, half * 1024:half * 1024 + 1024],
                                                 s2[:, half * 1024:half * 1024 + 1024], ACT.Copy
                                                 ).then_inc(lT_high, 1)
                        if kind == "m":
                            n = i - 13
                            eng.wait_ge(main.unit_used, done)
                            eng.wait_ge(lT_low, l * 2 + 2)
                            dst = s2 if n < 2 else s0
                            for c in range(4):
                                cc = 4 * (n % 2) + c
                                bm = C_BM + (8 if n < 2 else 0) + cc
                                ins = nc.scalar.activation(dst[:, cc * S:(cc + 1) * S],
                                                           pair[b][:, c * S:(c + 1) * S], ACT.Tanh, scale=0.5,
                                                           bias=cur[:, bm:bm + 1])
                            ins.then_inc(pair_read[b], 1)
                        if 2 * ATT0 <= p < 2 * (ATT0 + HEADS) and p % 2 == 0:
                            h = p // 2 - ATT0
                            for t in range(NT):
                                eng.wait_ge(max_ready, l * 16 + 2 * h + t + 1)
                                pr = probs[:, 0:768] if t == 1 else probs[:, 768:1152]
                                nc.scalar.activation(pr, pr, ACT.Exp, bias=nmax[:, t:t + 1],
                                                     accum_out=den[:, t:t + 1]).then_inc(exp_ready, 1)
                        if 2 * ATT0 < p < 2 * (ATT0 + HEADS) and p % 2 == 1:
                            h = p // 2 - ATT0
                            eng.wait_ge(pT_done, l * 8 + h + 1)
                            nc.scalar.activation(pT, pS[:, 0:1152], ACT.Copy).then_inc(pT_ready, 1)
                        if p == 38:
                            eng.wait_ge(pv_done, l * 8 + 8)
                            load_row(l)
                            eng.wait_ge(aT_done, l + 1)
                            nc.scalar.activation(att_h[:, :], pS[:, 0:1024], ACT.Copy).then_inc(aT_high, 1)
                        if kind == "pa":
                            half = i - 19
                            eng.wait_ge(mix_full, l * 2 + half + 1)
                            nc.scalar.activation(act_h[:, half * 1024:half * 1024 + 1024],
                                                 s0[:, half * 1024:half * 1024 + 1024], ACT.Copy, scale=0.5
                                                 ).then_inc(mix_high, 1)
                eng.wait_ge(h2_ready, l * 4 + 2)
                sum_squares()
                split_w(l, W_UNITS + 1)
                eng.wait_ge(h2_ready, l * 4 + 4)
                nc.scalar.activation(act_h[:, :], s0[:, 0:2048], ACT.Copy).then_inc(h2_high, 1)
                for half in range(2):
                    eng.wait_ge(h2T_done, l * 2 + half + 1)
                    nc.scalar.activation(s2[:, half * 1024:half * 1024 + 1024], pair[half][:, :], ACT.Copy
                                         ).then_inc(h2T_ready, 1)
                for t in range(NT):
                    eng.wait_ge(gneg_ready, l + 1)
                    nc.scalar.activation(rs[:, 6 + 2 * t:8 + 2 * t, :].rearrange("p a b -> p (a b)"),
                                         lg[:, t, 0:EG], ACT.Exp, bias=rs[:, 0, t:t + 1],
                                         accum_out=rs[:, 1, t:t + 1]).then_inc(gexp_ready, 1)
                eng.wait_ge(diff_ready, l + 1)
                nc.scalar.activation(rs[:, 3, :], rs[:, 2, :], ACT.Exp).then_inc(e2_ready, 1)
                moe(main, l, W_UNITS)
                eng.wait_ge(flag_ready, l + 1)
                settled(eng)
                more = eng.value_load(flag[0:1, 0:1], min_val=0, max_val=1)
                with eng.If(more > 0):
                    eng.wait_ge(main.unit_used, l * UNITS + UNITS + SLOTS)
                    with eng.Fori(0, MORE) as q:
                        n = l * MORE + q
                        for j in range(2):
                            split_high(over_flow, j, (n * NE + 1) * 16, n * M_UNITS + j + 1, j)
                        moe(over_flow, n, 0)
                    eng.wait_ge(over_flow.unit_used, (l + 1) * (MORE * M_UNITS) + SLOTS)
                    settled(eng)
                with eng.Else():
                    eng.sem_inc(over_flow.high_ready, M_UNITS * MORE)
                    for sm, k in ((over_flow.pt_ready, NE), (over_flow.he_high0, NE + 1),
                                  (over_flow.he_high1, NE + 1), (over_flow.tanh_ready, NE),
                                  (over_flow.g_low, NE), (over_flow.u_low, NE),
                                  (over_flow.ae_high, NE), (over_flow.y_high0, NE), (over_flow.y_high1, NE)):
                        eng.sem_inc(sm, k * MORE)
            eng.wait_ge(x_done, LAYERS + 1)
            sum_squares()
            load_row(LAYERS)
            eng.wait_ge(nrow_in, 16 * (LAYERS + 1))

        @block.gpsimd
        def _(pool_eng):
            eng = pool_eng
            for flow in (main, over_flow):
                eng.sem_inc(flow.low_pool, RAW)
            nc.gpsimd.memset(mhalf[:, :], -0.5).then_inc(pool_chain, 1)

            def split_low(flow, count, raw_slot, slot):
                eng.wait_ge(flow.high_ready, count)
                nc.gpsimd.tensor_tensor(low[:, slot, POOL_AT:UCOL], raw[:, raw_slot, POOL_AT:UCOL],
                                        high[:, slot, POOL_AT:UCOL].bitcast(f32), ALU.subtract
                                        ).then_inc(flow.low_pool, 1)

            def split_w(l, u):
                split_low(main, l * UNITS + u + 1, RAW_SLOT[u], u % SLOTS)

            def power(count, norm):
                eng.wait_ge(ss_ready, count)
                settled(eng)
                nc.gpsimd.tensor_scalar(rstd[:, :], ss[:, :], 1.0 / D, EPS, ALU.mult, ALU.add
                                        ).then_inc(pool_chain, 1)
                eng.wait_ge(pool_chain, norm + 2)
                nc.gpsimd.tensor_tensor(rstd[:, :], rstd[:, :], mhalf[:, :], ALU.pow).then_inc(rstd_ready, 1)

            with eng.Fori(0, LAYERS) as l:
                power(l * 4 + 2, l * 2)
                eng.wait_ge(xT_done, l * 2 + 2)
                settled(eng)
                nc.gpsimd.memset(upad[:, :, 0:3], 0.0).then_inc(pad_zero, 1)
                for u in range(W_UNITS + 1):
                    split_w(l, u)
                power(l * 4 + 4, l * 2 + 1)
                split_w(l, W_UNITS + 1)
                with eng.Fori(0, NE - 1) as e:
                    for j in range(2, E_UNITS + 2):
                        split_low(main, l * UNITS + e * E_UNITS + (W_UNITS + j + 1), j % RAW,
                                  (W_UNITS + j) % SLOTS)
                for u in range(UNITS - 4, UNITS):
                    split_w(l, u)
                eng.wait_ge(flag_ready, l + 1)
                settled(eng)
                more = eng.value_load(flag[0:1, 0:1], min_val=0, max_val=1)
                with eng.If(more > 0):
                    with eng.Fori(0, MORE * NE) as i:
                        for j in range(RAW):
                            split_low(over_flow, l * (MORE * M_UNITS) + i * RAW + (j + 1), j, j % SLOTS)
                with eng.Else():
                    eng.sem_inc(over_flow.low_pool, M_UNITS * MORE)
            power(LAYERS * 4 + 2, LAYERS * 2)

        @block.vector
        def _(dve_eng):
            eng = dve_eng
            chain = Chain(eng, dve_chain)
            for flow in (main, over_flow):
                eng.sem_inc(flow.low_dve, RAW)
                eng.sem_inc(flow.y_low0, 1)
                eng.sem_inc(flow.y_low1, 1)
            eng.sem_inc(x_done, 1)

            def split_low(flow, count, raw_slot, slot):
                eng.wait_ge(flow.high_ready, count)
                nc.vector.tensor_tensor(low[:, slot, 0:POOL_AT], raw[:, raw_slot, 0:POOL_AT],
                                        high[:, slot, 0:POOL_AT].bitcast(f32), ALU.subtract
                                        ).then_inc(flow.low_dve, 1)

            def split_w(l, u):
                split_low(main, l * UNITS + u + 1, RAW_SLOT[u], u % SLOTS)

            def slots_of(flow, e_col):
                for t in range(NT):
                    ins = nc.vector.tensor_scalar(pe_01[:, t, :], iota[:, :],
                                                  rank[:, t, ds(e_col, 1)], None, ALU.is_equal)
                ins.then_inc(flow.p_ready, 1)

            def moe(flow, l, first):
                def split(e, j):
                    split_low(flow, l * flow.units + e * E_UNITS + (first + j + 1), j, (first + j) % SLOTS)

                def low_he(e_next, half):
                    eng.wait_ge([flow.he_high0, flow.he_high1][half], l * (NE + 1) + e_next + 1)
                    c = slice(4 * half, 4 * half + 4)
                    nc.vector.tensor_tensor(he[:, c, CAP:P],
                                            bank[2 + half][:, 0:256].rearrange("p (c n) -> p c n", c=4),
                                            he[:, c, 0:CAP].bitcast(f32), ALU.subtract
                                            ).then_inc([flow.he_low0, flow.he_low1][half], 1)

                def expert(e, last):
                    split(e, 2)
                    split(e, 3)
                    eng.wait_ge(flow.g_low, l * NE + e + 1)
                    nc.vector.tensor_tensor(g_sum, g_low, bank[0][0:CAP, :], ALU.add).then_inc(flow.g_sum, 1)
                    eng.wait_ge(flow.tanh_ready, l * NE + e + 1)
                    nc.vector.scalar_tensor_tensor(tgate, tgate, 1.0, g_sum, ALU.add, ALU.mult
                                                   ).then_inc(flow.dve_chain, 1)
                    eng.wait_ge(flow.pt_ready, l * NE + e + 1)
                    nc.vector.tensor_copy(ws[:, :], bank[2][:, S:S + 1]).then_inc(flow.ws_ready, 1)
                    slots_of(flow, e + 1)
                    split(e, 4)
                    eng.wait_ge(flow.u_low, l * NE + e + 1)
                    nc.vector.tensor_tensor(u_sum, u_low, bank[1][0:CAP, :], ALU.add).then_inc(flow.u_sum, 1)
                    eng.wait_ge(flow.dve_chain, l * NE + e + 1)
                    eng.wait_ge(flow.u_sum, l * NE + e + 1)
                    nc.vector.scalar_tensor_tensor(act, tgate, 0.5, u_sum, ALU.mult, ALU.mult
                                                   ).then_inc(flow.act_ready, 1)
                    low_he(e + 1, 0)
                    eng.wait_ge(flow.ae_high, l * NE + e + 1)
                    nc.vector.tensor_tensor(ae[:, :, CAP:P],
                                            bank[0][:, 0:256].rearrange("p (c n) -> p c n", c=4),
                                            ae[:, :, 0:CAP].bitcast(f32), ALU.subtract
                                            ).then_inc(flow.ae_low, 1)
                    split(e, 5)
                    low_he(e + 1, 1)
                    if not last:
                        split(e + 1, 0)
                    for half in range(2):
                        eng.wait_ge([flow.y_high0, flow.y_high1][half], l * NE + e + 2)
                        eng.wait_ge(flow.ws_ready, l * NE + e + 1)
                        cols = slice(512 * half, 512 * half + 512)
                        nc.vector.scalar_tensor_tensor(y_l[:, cols], bank[1 + half], ws[:, 0:1],
                                                       y_h[:, cols].bitcast(f32), ALU.mult, ALU.subtract
                                                       ).then_inc([flow.y_low0, flow.y_low1][half], 1)
                    if not last:
                        split(e + 1, 1)

                settled(eng)
                nc.vector.memset(y_h.bitcast(f32), 0.0)
                nc.vector.memset(y_l.bitcast(f32), 0.0).then_inc(flow.y_zero, 1)
                slots_of(flow, 0)
                low_he(0, 0)
                low_he(0, 1)
                with eng.Fori(0, NE - 1) as e:
                    expert(e, False)
                expert(NE - 1, True)
                eng.wait_ge(flow.moe_done, l + 1)
                for t in range(NT):
                    nc.vector.tensor_tensor(xs[:, t, :], xs[:, t, :], pair[t][:, :], ALU.add
                                            ).then_inc(flow.x_added, 1)

            eng.wait_ge(mask_in, 16)
            nc.vector.tensor_copy(mask[:, :, :], s2[:, 0:768].rearrange("p (g n) -> p g n", g=GROUPS)
                                  ).then_inc(table_zero, 1)
            nc.vector.memset(ones[:, :], 1.0).then_inc(table_zero, 1)
            nc.vector.memset(g8[:, :, :], -3.0e38).then_inc(table_zero, 1)
            nc.vector.memset(e8[:, :, :], -3.0e38).then_inc(table_zero, 1)
            nc.vector.memset(rank[:, :, :], -1.0).then_inc(table_zero, 1)
            nc.vector.memset(pt_01.bitcast(f32), 0.0).then_inc(table_zero, 1)
            eng.wait_ge(table_zero, 6)
            eng.wait_ge(const_in, 96)

            with eng.Fori(0, LAYERS) as l:
                chain.at(l * DVE_LINKS)
                chain.link(nc.vector.tensor_copy(cur[:, :], smalls[:, ds(l, 1), :].rearrange("p o n -> p (o n)")))
                nc.vector.tensor_scalar(cur[:, C_BA:C_BX + 8], cur[:, C_BA:C_BX + 8], 0.5, None, ALU.mult
                                        ).then_inc(cur_ready, 1)
                nc.vector.tensor_scalar(cur[:, C_BM:C_BM + 16], cur[:, C_BM:C_BM + 16], 0.5, None, ALU.mult
                                        ).then_inc(cur_ready, 1)
                eng.wait_ge(rstd_ready, l * 2 + 1)
                for t in range(NT):
                    nc.vector.tensor_scalar(xn[:, t, :], xs[:, t, :], rstd[:, t:t + 1], None, ALU.mult
                                            ).then_inc(xn_ready, 1)
                lam = cur[:, C_LAM:C_LAM + 8]
                chain.link(nc.vector.tensor_scalar(sp[:, 0, :], lam, -1.0, None, ALU.mult))
                nc.vector.tensor_tensor(sp[:, 1, :], lam, sp[:, 0, :], ALU.max).then_inc(elam_ready, 1)
                for half in range(2):
                    split_w(l, half)
                    eng.wait_ge(hT_high, l * 8 + 4 * half + 4)
                    for c in range(4 * half, 4 * half + 4):
                        nc.vector.scalar_tensor_tensor(hT_l[:, c, :], pair[half][:, (c % 4) * S:(c % 4 + 1) * S],
                                                       cur[:, C_N1 + c:C_N1 + c + 1],
                                                       hT_h[:, c, :].bitcast(f32), ALU.mult, ALU.subtract
                                                       ).then_inc(hT_low, 1)
                eng.wait_ge(elam_ready, l * 2 + 2)
                ee, s_, s2_, acc = sp[:, 2, :], sp[:, 3, :], sp[:, 4, :], sp[:, 5, :]
                chain.link(nc.vector.tensor_scalar(s_, ee, 2.0, None, ALU.add))
                chain.link(nc.vector.reciprocal(s_, s_))
                chain.link(nc.vector.tensor_tensor(s_, s_, ee, ALU.mult))
                chain.link(nc.vector.tensor_tensor(s2_, s_, s_, ALU.mult))
                chain.link(nc.vector.tensor_scalar(acc, s2_, 1.0 / 17.0, None, ALU.mult))
                for odd in (15, 13, 11, 9, 7, 5, 3):
                    chain.link(nc.vector.scalar_tensor_tensor(acc, acc, 1.0 / odd, s2_, ALU.add, ALU.mult))
                chain.link(nc.vector.scalar_tensor_tensor(acc, acc, 1.0, s_, ALU.add, ALU.mult))
                chain.link(nc.vector.tensor_scalar(sp[:, 0, :], sp[:, 0, :], 0.0, None, ALU.max))
                chain.link(nc.vector.scalar_tensor_tensor(acc, acc, 2.0, sp[:, 0, :], ALU.mult, ALU.add))
                nc.vector.tensor_scalar(sp[:, 6, :], acc, -4.0, None, ALU.mult).then_inc(sp_ready, 1)
                nc.vector.tensor_scalar(sp[:, 7, :], acc, 4.0, None, ALU.mult).then_inc(sp_ready, 1)

                for u in range(2, W_UNITS + 1):
                    split_w(l, u)
                    for p in ([u - 1] if u < W_UNITS else [W_UNITS - 1, W_UNITS]):
                        i = GROUP_END.get(p)
                        kind = GROUP_KINDS[i] if i is not None else None
                        b = None if i is None else i % 2
                        done = None if i is None else l * UNITS + (p + SLOTS)
                        if kind == "u":
                            eng.wait_ge(u_ready, l * 2 + i + 1)
                            eng.wait_ge(pair_read[b], l * PAIR_READS[b] + (i // 2 + 1))
                            for tap in range(2, -1, -1):
                                for c in range(4 * i, 4 * i + 4):
                                    w = cur[:, C_CW + 8 * tap + c:C_CW + 8 * tap + c + 1]
                                    ins = nc.vector.scalar_tensor_tensor(conv[:, c, :], upad[:, c, tap:tap + S], w,
                                                                         conv[:, c, :], ALU.mult, ALU.add)
                                    if tap:
                                        ins.then_inc(dve_chain, 1)
                                        chain.n += 1
                                    else:
                                        ins.then_inc(conv_ready, 1)
                                if tap:
                                    eng.wait_ge(dve_chain, chain.base + chain.n)
                        if kind in ("q", "k"):
                            eng.wait_ge(main.unit_used, done)
                            for t in range(NT):
                                n = (i - 2) * NT + t
                                if n >= 2:
                                    eng.wait_ge(rotT_done, l * 12 + n - 1)
                                xq = pair[b][:, t * 512:(t + 1) * 512].rearrange("p (h n) -> p h n", h=HEADS)
                                a = v[:, 0, 512 + 512 * t:1024 + 512 * t].rearrange("p (h n) -> p h n", h=HEADS)
                                c_ = v[:, 1, 512 + 512 * t:1024 + 512 * t].rearrange("p (h n) -> p h n", h=HEADS)
                                cs = cos2[:, t, :].unsqueeze(1).to_broadcast([P, HEADS, HD])
                                sn = sin2[:, t, :].unsqueeze(1).to_broadcast([P, HEADS, HD])
                                nc.vector.tensor_tensor(a, xq, cs, ALU.mult).then_inc(dve_chain, 1)
                                nc.vector.tensor_tensor(c_[:, :, 0:32], xq[:, :, 32:64], sn[:, :, 0:32], ALU.mult
                                                        ).then_inc(dve_chain, 1)
                                nc.vector.tensor_tensor(c_[:, :, 32:64], xq[:, :, 0:32], sn[:, :, 32:64], ALU.mult
                                                        ).then_inc(pair_read[b] if t else dve_chain, 1)
                                chain.n += 2 if t else 3
                                eng.wait_ge(dve_chain, chain.base + chain.n)
                                if t:
                                    eng.wait_ge(pair_read[b], l * PAIR_READS[b] + (i // 2 + 1))
                                nc.vector.tensor_tensor(a, a, c_, ALU.add).then_inc(rot_ready, 1)
                        if p == 9:
                            eng.wait_ge(i_ready, l * 8 + 8)
                            eng.wait_ge(conv_ready, l * 8 + 8)
                            chain.link(nc.vector.scalar_tensor_tensor(s3[:, :], s3[:, :], 1.0, s1[:, :],
                                                                      ALU.add, ALU.mult))
                        if p == 11:
                            eng.wait_ge(decay_ready, l * 8 + 8)
                            eng.wait_ge(t_ready, l * 8 + 8)
                            chain.link(nc.vector.tensor_tensor(s1[:, :], s0[:, 0:2048], s0[:, 0:2048], ALU.mult))
                            nc.vector.scalar_tensor_tensor(s2[:, :], s1[:, :], 1.0, s2[:, :], ALU.add, ALU.mult
                                                           ).then_inc(v_ready, 1)
                        if p == 13:
                            eng.wait_ge(root_ready, l + 1)
                            chain.link(nc.vector.tensor_tensor(s3[:, :], s3[:, :], s2[:, :], ALU.mult))
                            for c in range(8):
                                nc.vector.tensor_tensor_scan(rec[:, c * S:(c + 1) * S], decay[:, c, :],
                                                             s3[:, c * S:(c + 1) * S], 0.0, ALU.mult, ALU.add
                                                             ).then_inc(rec_ready, 1)
                        if kind == "g":
                            half = i - ATT0
                            cols = slice(half * 1024, half * 1024 + 1024)
                            eng.wait_ge(g_ready, l * 2 + half + 1)
                            eng.wait_ge(pair_read[b], l * PAIR_READS[b] + (i // 2 + 1))
                            chain.link(nc.vector.tensor_scalar(s2[:, cols], s2[:, cols], 0.044715, 1.0,
                                                               ALU.mult, ALU.add))
                            nc.vector.tensor_tensor(s2[:, cols], s2[:, cols], s0[:, cols], ALU.mult
                                                    ).then_inc(g_inner, 1)
                            eng.wait_ge(g_tanh, l * 2 + half + 1)
                            eng.wait_ge(rec_ready, l * 8 + 8)
                            chain.link(nc.vector.scalar_tensor_tensor(s0[:, cols], s2[:, cols], 1.0, s0[:, cols],
                                                                      ALU.add, ALU.mult))
                            nc.vector.scalar_tensor_tensor(s2[:, cols], s0[:, cols], 0.5, rec[:, cols],
                                                           ALU.mult, ALU.mult).then_inc(lru_full, 1)
                            eng.wait_ge(lT_high, l * 2 + half + 1)
                            nc.vector.tensor_tensor(lru_l[:, cols], s2[:, cols], lru_h[:, cols].bitcast(f32),
                                                    ALU.subtract).then_inc(lT_low, 1)
                        if kind == "pl":
                            cols = slice((i - 17) * 1024, (i - 17) * 1024 + 1024)
                            eng.wait_ge(main.unit_used, done)
                            eng.wait_ge(pair_read[1], l * PAIR_READS[1] + 8)
                            eng.wait_ge(pair_read[0], l * PAIR_READS[0] + 8)
                            nc.vector.scalar_tensor_tensor(s2[:, cols], s2[:, cols], 1.0, pair[b][:, :],
                                                           ALU.add, ALU.mult).then_inc(pair_read[b], 1)
                        if 2 * ATT0 + 2 <= p <= 2 * ATT0 + 16 and p % 2 == 0:
                            h = (p - 2) // 2 - ATT0
                            eng.wait_ge(exp_ready, l * 16 + 2 * h + 2)
                            chain.link(nc.vector.reciprocal(rden[:, :], den[:, :]))
                            eng.wait_ge(pv_done, l * 8 + h + 1)
                            for t in range(NT):
                                nc.vector.tensor_scalar(attn[:, t, h * HD:(h + 1) * HD],
                                                        pO[:, t * HD:(t + 1) * HD], rden[:, t:t + 1], None,
                                                        ALU.mult).then_inc(attn_ready, 1)
                        if 2 * ATT0 <= p < 2 * (ATT0 + HEADS) and p % 2 == 0:
                            h = p // 2 - ATT0
                            eng.wait_ge(qk_done, l * 8 + h + 1)
                            if h:
                                eng.wait_ge(pT_done, l * 8 + h)
                            for t in (1, 0):
                                w = S if t else P
                                cols = slice(0, 768) if t else slice(768, 1152)
                                pr = probs[:, cols]
                                chain.link(nc.vector.scalar_tensor_tensor(
                                    pr.rearrange("p (g n) -> p g n", g=GROUPS),
                                    pS[:, cols].rearrange("p (g n) -> p g n", g=GROUPS), HD ** -0.5,
                                    mask[:, :, S - w:S], ALU.mult, ALU.add))
                            for t in range(NT):
                                pr = probs[:, 0:768] if t == 1 else probs[:, 768:1152]
                                nc.vector.tensor_reduce(nmax[:, t:t + 1], pr, AX.X, ALU.max, negate=True
                                                        ).then_inc(max_ready, 1)
                        if p == 38:
                            eng.wait_ge(aT_high, l + 1)
                            nc.vector.tensor_tensor(att_l[:, :], pS[:, 0:1024], att_h[:, :].bitcast(f32),
                                                    ALU.subtract).then_inc(aT_low, 1)
                        if kind == "pa":
                            half = i - 19
                            cols = slice(half * 1024, half * 1024 + 1024)
                            eng.wait_ge(main.unit_used, done)
                            eng.wait_ge(pair_read[0], l * PAIR_READS[0] + 9)
                            nc.vector.scalar_tensor_tensor(s0[:, cols], s0[:, cols], 1.0, pair[b][:, :],
                                                           ALU.add, ALU.mult).then_inc(pair_read[b], 1)
                            eng.wait_ge(pair_read[b], l * PAIR_READS[b] + (i // 2 + 1))
                            nc.vector.tensor_tensor(s0[:, cols], s0[:, cols], s2[:, cols], ALU.add
                                                    ).then_inc(mix_full, 1)
                            eng.wait_ge(mix_high, l * 2 + half + 1)
                            nc.vector.scalar_tensor_tensor(act_l[:, cols], s0[:, cols], 0.5,
                                                           act_h[:, cols].bitcast(f32), ALU.mult, ALU.subtract
                                                           ).then_inc(mix_low, 1)
                        if kind == "wo":
                            n = i - 21
                            eng.wait_ge(main.unit_used, done)
                            nc.vector.tensor_tensor(xs[:, :, n * 512:(n + 1) * 512],
                                                    xs[:, :, n * 512:(n + 1) * 512],
                                                    pair[b][:, :].rearrange("p (t n) -> p t n", t=NT), ALU.add
                                                    ).then_inc(h2_ready, 1)
                eng.wait_ge(rstd_ready, l * 2 + 2)
                eng.wait_ge(nrow_in, l * 16 + 16)
                for t in range(NT):
                    nc.vector.scalar_tensor_tensor(h2[:, t, :], xs[:, t, :], rstd[:, t:t + 1], nrow,
                                                   ALU.mult, ALU.mult).then_inc(h2_ready, 1)
                split_w(l, W_UNITS + 1)
                eng.wait_ge(h2_high, l + 1)
                nc.vector.tensor_tensor(act_l[:, :], s0[:, 0:2048], act_h[:, :].bitcast(f32), ALU.subtract
                                        ).then_inc(h2_low, 1)
                eng.wait_ge(logits_done, l + 1)
                chain.link(nc.vector.tensor_tensor(
                    lg[:, :, :], pO[:, 0:40].rearrange("p (t n) -> p t n", t=NT),
                    cur[:, C_RB:C_RB + 20].unsqueeze(1).to_broadcast([P, NT, 20]), ALU.add))
                chain.link(nc.vector.tensor_copy(g8[:, :, 0:EG], lg[:, :, 0:EG]))
                for t in range(NT):
                    settled(eng)
                    chain.link(nc.vector.max(gm[:, t, :], g8[:, t, :]))
                    settled(eng)
                    chain.link(nc.vector.max_index(gi[:, t, :], gm[:, t, :], g8[:, t, :]))
                nc.vector.tensor_scalar(rs[:, 0, :], gm[:, :, 0:1].rearrange("p t o -> p (t o)"), -1.0, None,
                                        ALU.mult).then_inc(gneg_ready, 1)
                chain.link(nc.vector.tensor_copy(gf[:, :, :], gi[:, :, :]))
                for t in range(NT):
                    chain.link(nc.vector.tensor_scalar(goh[:, t, :], iota[:, 0:EG], gf[:, t, 0:1], None,
                                                       ALU.is_equal))
                for t in range(NT):
                    chain.link(nc.vector.tensor_tensor(
                        r16[:, t, :].rearrange("p (g j) -> p g j", g=EG),
                        lg[:, t, EG:20].rearrange("p (g j) -> p g j", g=EG),
                        goh[:, t, :].unsqueeze(2).to_broadcast([P, EG, EG]), ALU.mult))
                    chain.link(nc.vector.tensor_reduce(
                        e8[:, t, 0:EG], r16[:, t, :].rearrange("p (g j) -> p j g", g=EG), AX.X, ALU.add))
                    settled(eng)
                    chain.link(nc.vector.max(em[:, t, :], e8[:, t, :]))
                    settled(eng)
                    chain.link(nc.vector.max_index(ei[:, t, :], em[:, t, :], e8[:, t, :]))
                nc.vector.tensor_tensor(rs[:, 2, :], em[:, :, 1:2].rearrange("p t o -> p (t o)"),
                                        em[:, :, 0:1].rearrange("p t o -> p (t o)"), ALU.subtract
                                        ).then_inc(diff_ready, 1)
                chain.link(nc.vector.tensor_copy(ef[:, :, :], ei[:, :, :]))
                for t in range(NT):
                    chain.link(nc.vector.tensor_scalar(oh1[:, t, :], iota[:, 0:EG], ef[:, t, 0:1], None,
                                                       ALU.is_equal))
                    chain.link(nc.vector.tensor_scalar(oh2[:, t, :], iota[:, 0:EG], ef[:, t, 1:2], None,
                                                       ALU.is_equal))
                chain.link(nc.vector.tensor_tensor(r16[:, :, 0:EG], oh1[:, :, :], oh2[:, :, :], ALU.add))
                for t in range(NT):
                    nc.vector.tensor_tensor(sel[:, t, :].rearrange("p (g j) -> p g j", g=EG),
                                            goh[:, t, :].unsqueeze(2).to_broadcast([P, EG, EG]),
                                            r16[:, t, 0:EG].unsqueeze(1).to_broadcast([P, EG, EG]), ALU.mult
                                            ).then_inc(sel_ready, 1)
                eng.wait_ge(e2_ready, l + 1)
                eng.wait_ge(gexp_ready, l * 2 + 2)
                chain.link(nc.vector.tensor_scalar(rs[:, 4, :], rs[:, 3, :], 1.0, None, ALU.add))
                chain.link(nc.vector.tensor_tensor(rs[:, 4, :], rs[:, 4, :], rs[:, 1, :], ALU.mult))
                chain.link(nc.vector.reciprocal(rs[:, 4, :], rs[:, 4, :]))
                chain.link(nc.vector.tensor_tensor(rs[:, 5, :], rs[:, 4, :], rs[:, 3, :], ALU.mult))
                for t in range(NT):
                    chain.link(nc.vector.tensor_scalar(oh1[:, t, :], oh1[:, t, :], rs[:, 4, t:t + 1], None,
                                                       ALU.mult))
                    chain.link(nc.vector.scalar_tensor_tensor(oh1[:, t, :], oh2[:, t, :], rs[:, 5, t:t + 1],
                                                              oh1[:, t, :], ALU.mult, ALU.add))
                    nc.vector.tensor_tensor(comb[:, t, :].rearrange("p (g j) -> p g j", g=EG),
                                            goh[:, t, :].unsqueeze(2).to_broadcast([P, EG, EG]),
                                            oh1[:, t, :].unsqueeze(1).to_broadcast([P, EG, EG]), ALU.mult
                                            ).then_inc(sel_ready, 1)
                eng.wait_ge(rank_done, l + 1)
                eng.wait_ge(sel_ready, l * 4 + 4)
                chain.link(nc.vector.scalar_tensor_tensor(
                    rank[:, :, 0:NE], pO[:, 64:96].rearrange("p (t n) -> p t n", t=NT), 1.0, sel[:, :, :],
                    ALU.add, ALU.mult))
                chain.link(nc.vector.tensor_scalar(rank[:, :, 0:NE], rank[:, :, 0:NE], -1.0, None, ALU.add))
                chain.link(nc.vector.tensor_reduce(over[:, :], pO[:, 128:128 + NE], AX.X, ALU.max))
                nc.vector.tensor_scalar(flag[:, :], over[:, :], float(CAP) + 0.5, None, ALU.is_ge
                                        ).then_inc(flag_ready, 1)
                assert chain.n == DVE_LINKS, f"DVE_LINKS = {chain.n}"
                moe(main, l, W_UNITS)
                eng.wait_ge(flag_ready, l + 1)
                settled(eng)
                more = eng.value_load(flag[0:1, 0:1], min_val=0, max_val=1)
                with eng.If(more > 0):
                    eng.wait_ge(main.x_added, l * 2 + 2)
                    settled(eng)
                    with eng.Fori(0, MORE) as q:
                        n = l * MORE + q
                        nc.vector.tensor_scalar(rank[:, :, :], rank[:, :, :], -float(CAP), None, ALU.add
                                                ).then_inc(rank_moved, 1)
                        for j in range(2):
                            split_low(over_flow, n * M_UNITS + j + 1, j, j)
                        eng.wait_ge(rank_moved, n + 1)
                        moe(over_flow, n, 0)
                        eng.wait_ge(over_flow.x_added, n * 2 + 2)
                    eng.sem_inc(x_done, 1)
                with eng.Else():
                    eng.sem_inc(rank_moved, MORE)
                    for sm, k in ((over_flow.low_dve, M_UNITS), (over_flow.p_ready, NE + 1),
                                  (over_flow.ws_ready, NE), (over_flow.he_low0, NE + 1),
                                  (over_flow.he_low1, NE + 1), (over_flow.act_ready, NE), (over_flow.ae_low, NE),
                                  (over_flow.g_sum, NE), (over_flow.u_sum, NE),
                                  (over_flow.y_low0, NE), (over_flow.y_low1, NE), (over_flow.y_zero, 1),
                                  (over_flow.x_added, 2), (over_flow.dve_chain, NE)):
                        eng.sem_inc(sm, k * MORE)
                    eng.wait_ge(main.x_added, l * 2 + 2)
                    eng.sem_inc(x_done, 1)
            eng.wait_ge(rstd_ready, LAYERS * 2 + 1)
            eng.wait_ge(nrow_in, 16 * (LAYERS + 1))
            for t in range(NT):
                nc.vector.scalar_tensor_tensor(xn[:, t, :], xs[:, t, :], rstd[:, t:t + 1], nrow, ALU.mult,
                                               ALU.mult).then_inc(out_done, 1)

        @block.tensor
        def _(pe_eng):
            eng = pe_eng
            mm = nc.tensor.matmul
            for flow in (main, over_flow):
                eng.sem_inc(flow.unit_used, SLOTS)

            def unit_there(flow, count):
                eng.wait_ge(flow.high_ready, count)
                eng.wait_ge(flow.low_dve, count + RAW)
                eng.wait_ge(flow.low_pool, count + RAW)

            def tok_unit(slot, xh, xl, outs, k0, start, stop):
                for t in range(len(outs)):
                    for k in range(4):
                        w = slice(k * 512, (k + 1) * 512)
                        mm(outs[t], xh(k0 + k, t), high[:, slot, w], start=start and k == 0, stop=False)
                        mm(outs[t], xh(k0 + k, t), low[:, slot, w], start=False, stop=False)
                        ins = mm(outs[t], xl(k0 + k, t), high[:, slot, w], start=False, stop=stop and k == 3)
                return ins

            def feat_unit(slot, xh, xl, out, ktiles):
                width = UCOL // ktiles
                for f in range(width // P):
                    o = out[:, f * S:(f + 1) * S]
                    for k in range(ktiles):
                        w = slice(k * width + f * P, k * width + (f + 1) * P)
                        mm(o, high[:, slot, w], xh[:, k, :], start=k == 0, stop=False)
                        mm(o, high[:, slot, w], xl[:, k, :], start=False, stop=False)
                        ins = mm(o, low[:, slot, w], xh[:, k, :], start=False, stop=k == ktiles - 1)
                return ins

            def scatter(flow, l, e, stop):
                for half in range(2):
                    eng.wait_ge([flow.y_high0, flow.y_high1][half], l * NE + e + 1)
                    eng.wait_ge([flow.y_low0, flow.y_low1][half], l * NE + e + 1)
                for t in range(NT):
                    for half in range(2):
                        cols = slice(512 * half, 512 * half + 512)
                        mm(pair[t][:, cols], pt_01[:, t * P:(t + 1) * P], y_h[:, cols], start=False, stop=False)
                        ins = mm(pair[t][:, cols], pt_01[:, t * P:(t + 1) * P], y_l[:, cols], start=False,
                                 stop=stop)
                return ins

            def gather(flow, l, e_next, half, chunks=range(4), done=True):
                for c in (4 * half + c for c in chunks):
                    n = 0
                    for t in range(NT):
                        for part in (h2_h, h2_l):
                            ins = mm(bank[2 + half][:, (c % 4) * CAP:(c % 4 + 1) * CAP],
                                     part[:, t, c * P:(c + 1) * P], pe_01[:, t, 0:CAP], start=n == 0,
                                     stop=n == 3)
                            n += 1
                if done:
                    ins.then_inc([flow.he_done0, flow.he_done1][half], 1)

            def moe(flow, l, first):
                def unit(e, j, x, out, k0, start, stop):
                    slot = (first + j) % SLOTS
                    unit_there(flow, l * flow.units + e * E_UNITS + (first + j + 1))
                    for k in range(4):
                        w = slice(k * 512, (k + 1) * 512)
                        mm(out, x[:, k0 + k, :], high[:, slot, w], start=start and k == 0, stop=False)
                        ins = mm(out, x[:, k0 + k, :], low[:, slot, w], start=False, stop=stop and k == 3)
                    ins.then_inc(flow.unit_used, 1)

                eng.wait_ge(flow.y_zero, l + 1)
                for t in range(NT):
                    for half in range(2):
                        mm(pair[t][:, 512 * half:512 * half + 512], pt_01[:, 0:P], y_h[:, 0:512], start=True,
                           stop=False)
                eng.wait_ge(flow.p_ready, l * (NE + 1) + 1)
                gather(flow, l, 0, 0)
                gather(flow, l, 0, 1)
                with eng.Fori(0, NE) as e:
                    for half in range(2):
                        eng.wait_ge([flow.he_high0, flow.he_high1][half], l * (NE + 1) + e + 1)
                        eng.wait_ge([flow.he_low0, flow.he_low1][half], l * (NE + 1) + e + 1)
                        unit(e, half, he, bank[0], 4 * half, half == 0, half == 1)
                        if half == 0:
                            scatter(flow, l, e, False)
                    for t in range(NT):
                        nc.tensor.transpose(bank[2][:, t * P:(t + 1) * P], pe_01[:, t, :].bitcast(f32),
                                            ident[:, :])
                    for t in range(NT):
                        ins = mm(bank[2][:, S:S + 1], pe_01[:, t, :].bitcast(f32), comb[:, t, ds(e, 1)],
                                 start=t == 0, stop=t == NT - 1)
                    ins.then_inc(flow.pt_done, 1)
                    for half in range(2):
                        unit(e, 2 + half, he, bank[1], 4 * half, half == 0, half == 1)
                    eng.wait_ge(flow.p_ready, l * (NE + 1) + e + 2)
                    eng.wait_ge(flow.pt_ready, l * NE + e + 1)
                    eng.wait_ge(flow.ws_ready, l * NE + e + 1)
                    gather(flow, l, e + 1, 0)
                    gather(flow, l, e + 1, 1, (0, 1), False)
                    eng.wait_ge(flow.act_ready, l * NE + e + 1)
                    settled(eng)
                    for c in range(4):
                        ins = nc.tensor.transpose(bank[0][:, c * CAP:(c + 1) * CAP], act[:, c * P:(c + 1) * P],
                                                  ident[0:CAP, 0:CAP])
                    ins.then_inc(flow.aeT_done, 1)
                    gather(flow, l, e + 1, 1, (2, 3))
                    eng.wait_ge(flow.ae_high, l * NE + e + 1)
                    eng.wait_ge(flow.ae_low, l * NE + e + 1)
                    for half in range(2):
                        if half:
                            eng.wait_ge(flow.he_high0, l * (NE + 1) + e + 2)
                            eng.wait_ge(flow.he_low0, l * (NE + 1) + e + 2)
                        unit(e, 4 + half, ae, bank[1 + half], 0, True, True)
                scatter(flow, l, NE, True).then_inc(flow.moe_done, 1)

            eng.wait_ge(const_in, 96)
            eng.wait_ge(table_zero, 6)
            with eng.Fori(0, LAYERS) as l:
                for half in range(2):
                    eng.wait_ge(xn_ready, l * 2 + 2)
                    for c in range(4):
                        for t in range(NT):
                            ins = nc.tensor.transpose(pair[half][:, c * S + t * P:c * S + (t + 1) * P],
                                                      xn[:, t, (4 * half + c) * P:(4 * half + c + 1) * P],
                                                      ident[:, :])
                    ins.then_inc(xT_done, 1)
                for i in range(NG):
                    kind, b = GROUP_KINDS[i], i % 2
                    outs = [pair[b][:, 0:512], pair[b][:, 512:1024]]
                    head = i - ATT0
                    if i >= 2:
                        eng.wait_ge(pair_read[b], l * PAIR_READS[b] + i // 2)
                    if 0 <= head < HEADS:
                        if head == 0:
                            eng.wait_ge(qkT_ready, l * 12 + 12)
                            eng.wait_ge(r_ready, l * 8 + 8)
                            eng.wait_ge(i_ready, l * 8 + 8)
                        else:
                            eng.wait_ge(pT_ready, l * 8 + head)
                        hp = slice((head % 2) * HD, (head % 2) * HD + HD)
                        for g in range(GROUPS):
                            c = 4 * g + head // 2
                            mm(pS[:, g * S:(g + 1) * S], qT[hp, c, P:S], kT[hp, c, :], start=True, stop=True)
                        for g in range(GROUPS):
                            c = 4 * g + head // 2
                            ins = mm(pS[:, 768 + g * P:768 + (g + 1) * P], qT[hp, c, 0:P], kT[hp, c, 0:P],
                                     start=True, stop=True)
                        ins.then_inc(qk_done, 1)
                    for n in range(GROUP_UNITS[i]):
                        u = GROUP_START[i] + n
                        unit_there(main, l * UNITS + u + 1)
                        last = n == GROUP_UNITS[i] - 1
                        if i == 0 and n == 0:
                            eng.wait_ge(hT_high, l * 8 + 8)
                            eng.wait_ge(hT_low, l * 8 + 8)
                        if kind in ("u", "g", "m"):
                            ins = feat_unit(u % SLOTS, hT_h, hT_l, outs[n], KD)
                        elif kind in ("q", "k", "v"):
                            ins = tok_unit(u % SLOTS, lambda k, t: hT_h[:, k, t * P:(t + 1) * P],
                                           lambda k, t: hT_l[:, k, t * P:(t + 1) * P], outs, 4 * n, n == 0, last)
                        elif kind == "pl":
                            if n == 0:
                                eng.wait_ge(lT_high, l * 2 + 2)
                                eng.wait_ge(lT_low, l * 2 + 2)
                            ins = feat_unit(u % SLOTS, lT_h, lT_l, outs[n], KD)
                        elif kind == "pa":
                            eng.wait_ge(aT_high, l + 1)
                            eng.wait_ge(aT_low, l + 1)
                            ins = feat_unit(u % SLOTS, aT_h, aT_l, pair[b], 4)
                        else:
                            eng.wait_ge(mix_high, l * 2 + n + 1)
                            eng.wait_ge(mix_low, l * 2 + n + 1)
                            ins = tok_unit(u % SLOTS, lambda k, t: hT_h[:, k, t * P:(t + 1) * P],
                                           lambda k, t: hT_l[:, k, t * P:(t + 1) * P], outs, 4 * n, n == 0, last)
                        ins.then_inc(main.unit_used, 1)
                        p = u + 1
                        if 5 <= p <= 8:
                            for c in range(2 * (p - 5), 2 * (p - 5) + 2):
                                if c == 0:
                                    eng.wait_ge(bd_in, l * 16 + 16)
                                eng.wait_ge(conv_ready, l * 8 + c + 1)
                                if c >= 3:
                                    eng.wait_ge(r_ready, l * 8 + c - 2)
                                    eng.wait_ge(i_ready, l * 8 + c - 2)
                                mm(pS[:, (c % 3) * 512:(c % 3) * 512 + S], bd[:, 0, c, :], conv[:, c, :],
                                   start=True, stop=True)
                                mm(pS[:, (c % 3) * 512 + S:(c % 3) * 512 + 2 * S], bd[:, 1, c, :], conv[:, c, :],
                                   start=True, stop=True).then_inc(gate_mm, 1)
                        for tile in range(NT):
                            j = GROUP_END.get(p - 1 - tile)
                            if j is not None and GROUP_KINDS[j] in "qk":
                                m = (j - 2) * NT + tile
                                eng.wait_ge(rot_ready, l * 12 + m + 1)
                                if m:
                                    eng.wait_ge(qkT_ready, l * 12 + m)
                                for c in range(4):
                                    ins = nc.tensor.transpose(
                                        pO[:, c * P:(c + 1) * P],
                                        v[:, 0, 512 + 512 * tile + c * P:512 + 512 * tile + (c + 1) * P],
                                        ident[:, :])
                                ins.then_inc(rotT_done, 1)
                        if 0 <= head < HEADS and n == 0:
                            eng.wait_ge(exp_ready, l * 16 + 2 * head + 2)
                            for blk in range(9):
                                ins = nc.tensor.transpose(pS[:, blk * P:(blk + 1) * P],
                                                          probs[:, blk * P:(blk + 1) * P], ident[:, :])
                            ins.then_inc(pT_done, 1)
                        if 0 <= head < HEADS and n == 1:
                            eng.wait_ge(pT_ready, l * 8 + head + 1)
                            if head == 0:
                                eng.wait_ge(pair_read[0], l * PAIR_READS[0] + 6)
                                eng.wait_ge(pair_read[1], l * PAIR_READS[1] + 5)
                            else:
                                eng.wait_ge(attn_ready, l * 16 + 2 * head)
                            for blk in range(6):
                                g, kb = blk // 2, blk % 2
                                mm(pO[:, HD:2 * HD], pT[:, blk * P:(blk + 1) * P],
                                   v[:, kb, g * 512 + head * HD:g * 512 + (head + 1) * HD],
                                   start=blk == 0, stop=blk == 5)
                            for g in range(GROUPS):
                                ins = mm(pO[:, 0:HD], pT[:, 768 + g * P:768 + (g + 1) * P],
                                         v[:, 0, g * 512 + head * HD:g * 512 + (head + 1) * HD],
                                         start=g == 0, stop=g == GROUPS - 1)
                            ins.then_inc(pv_done, 1)
                        if p == 38:
                            eng.wait_ge(attn_ready, l * 16 + 16)
                            for c in range(4):
                                for t in range(NT):
                                    ins = nc.tensor.transpose(pS[:, c * S + t * P:c * S + (t + 1) * P],
                                                              attn[:, t, c * P:(c + 1) * P], ident[:, :])
                            ins.then_inc(aT_done, 1)
                eng.wait_ge(h2_ready, l * 4 + 4)
                for half in range(2):
                    for c in range(4):
                        for t in range(NT):
                            ins = nc.tensor.transpose(pair[half][:, c * S + t * P:c * S + (t + 1) * P],
                                                      h2[:, t, (4 * half + c) * P:(4 * half + c + 1) * P],
                                                      ident[:, :])
                    ins.then_inc(h2T_done, 1)
                eng.wait_ge(h2T_ready, l * 2 + 2)
                for t in range(NT):
                    for k in range(KD):
                        ins = mm(pO[:, t * 20:(t + 1) * 20], h2T[:, k, t * P:(t + 1) * P],
                                 cur[:, C_RW + 20 * k:C_RW + 20 * (k + 1)], start=k == 0, stop=k == KD - 1)
                ins.then_inc(logits_done, 1)
                eng.wait_ge(sel_ready, l * 4 + 2)
                mm(pO[:, 64:80], tri[:, :], sel[:, 0, :], start=True, stop=True)
                mm(pO[:, 80:96], ones[:, :], sel[:, 0, :], start=True, stop=False)
                mm(pO[:, 80:96], tri[:, :], sel[:, 1, :], start=False, stop=True)
                mm(pO[:, 128:144], ones[:, :], sel[:, 0, :], start=True, stop=False)
                mm(pO[:, 128:144], ones[:, :], sel[:, 1, :], start=False, stop=True).then_inc(rank_done, 1)
                eng.wait_ge(sel_ready, l * 4 + 4)
                eng.wait_ge(h2_low, l + 1)
                moe(main, l, W_UNITS)
                eng.wait_ge(flag_ready, l + 1)
                settled(eng)
                more = eng.value_load(flag[0:1, 0:1], min_val=0, max_val=1)
                with eng.If(more > 0):
                    eng.wait_ge(main.x_added, l * 2 + 2)
                    settled(eng)
                    with eng.Fori(0, MORE) as q:
                        n = l * MORE + q
                        moe(over_flow, n, 0)
                        eng.wait_ge(over_flow.x_added, n * 2 + 2)
                        settled(eng)
                with eng.Else():
                    for sm, k in ((over_flow.unit_used, M_UNITS), (over_flow.pt_done, NE),
                                  (over_flow.he_done0, NE + 1), (over_flow.he_done1, NE + 1),
                                  (over_flow.aeT_done, NE), (over_flow.moe_done, 1)):
                        eng.sem_inc(sm, k * MORE)


def kernel(**inputs):
    import concourse.bacc as bacc
    from concourse.bass_utils import run_bass_kernel_spmd as run

    def arr(name):
        return np.ascontiguousarray(inputs[name])

    w_in, wpa, wpl, wo = arr("w_in"), arr("w_proj_attn"), arr("w_proj_lru"), arr("w_out")
    wg, wu, wd = arr("expert_w_gate"), arr("expert_w_up"), arr("expert_w_down")
    stream = np.empty((LAYERS * UNITS, P, UCOL), np.float32)

    def k_units(row, w):
        stream[row:row + 2] = w.reshape(2, 4, P, 512).transpose(0, 2, 1, 3).reshape(2, P, UCOL)

    def f_units(row, w):
        stream[row:row + 2] = w.reshape(KD, P, 2, 256).transpose(2, 1, 0, 3).reshape(2, P, UCOL)

    def n_units(row, w):
        stream[row:row + 2] = w.reshape(4, P, 2, 512).transpose(2, 1, 0, 3).reshape(2, P, UCOL)

    A = 1536
    u0, g0, m0 = 3 * A, 3 * A + D, 3 * A + 2 * D
    cols = ([u0, u0 + 512] + [n * 512 for n in range(9)] + [g0, g0 + 512]
            + [m0 + D, m0 + D + 512, m0, m0 + 512])
    for l in range(LAYERS):
        row = l * UNITS
        for kind, c in zip(GROUP_KINDS, cols):
            (k_units if kind in "qkv" else f_units)(row, w_in[l][:, c:c + 512])
            row += 2
        for n in range(2):
            f_units(row, wpl[l][:, n * 512:(n + 1) * 512])
            row += 2
        n_units(row, wpa[l])
        row += 2
        for n in range(2):
            k_units(row, wo[l][:, n * 512:(n + 1) * 512])
            row += 2
        for e in range(NE):
            k_units(row, wg[l, e])
            k_units(row + 2, wu[l, e])
            n_units(row + 4, wd[l, e])
            row += 6

    small = np.zeros((P, LAYERS, SMALL), np.float32)

    def put(col, a):
        a = a.reshape(LAYERS, -1, P)
        small[:, :, col:col + a.shape[1]] = a.transpose(2, 0, 1)

    for col, name in ((C_N1, "norm1_scale"), (C_BA, "lru_ba"), (C_BX, "lru_bx"), (C_LAM, "lru_lambda"),
                      (C_CB, "conv_b"), (C_CW, "conv_w"), (C_BM, "b_merge")):
        put(col, arr(name))
    rw = np.concatenate([arr("router_group_w"), arr("router_expert_w")], axis=2)
    small[:, :, C_RW:C_RW + 160] = rw.reshape(LAYERS, KD, P, 20).transpose(2, 0, 1, 3).reshape(P, LAYERS, 160)
    small[:, :, C_RB:C_RB + EG] = arr("router_group_b")[None]
    small[:, :, C_RB + EG:C_RB + 20] = arr("router_expert_b")[None]

    blockdiag = np.zeros((LAYERS, P, 2, 8, P), np.float32)
    for n, name in enumerate(("lru_wa", "lru_wx")):
        w = arr(name).reshape(LAYERS, 8, 2, HD, HD)
        for b in range(2):
            blockdiag[:, b * HD:(b + 1) * HD, n, :, b * HD:(b + 1) * HD] = w[:, :, b].transpose(0, 2, 1, 3)

    norm_rows = np.empty((LAYERS + 1, P, D), np.float32)
    norm_rows[:LAYERS] = arr("norm2_scale")[:, None, :]
    norm_rows[LAYERS] = arr("final_norm_scale")[None, :]

    tables = np.zeros((P, 768), np.float32)
    tables[:, 0:128] = np.eye(P, dtype=np.float32)
    tables[:, 128:256] = np.triu(np.ones((P, P), np.float32), 1)
    tables[:, 256:384] = np.tile(np.arange(CAP, dtype=np.float32), 2)[None]
    inv = (10000.0 ** (-np.arange(0, HD, 2, dtype=np.float32) / np.float32(HD))).astype(np.float32)
    ang = (np.arange(S, dtype=np.float32)[:, None] * inv[None, :]).astype(np.float32)
    cos, sin = np.cos(ang).astype(np.float32), np.sin(ang).astype(np.float32)
    tables[:, 512:640] = np.concatenate([cos, cos], 1).reshape(NT, P, HD).transpose(1, 0, 2).reshape(P, 128)
    tables[:, 640:768] = np.concatenate([-sin, sin], 1).reshape(NT, P, HD).transpose(1, 0, 2).reshape(P, 128)
    dist = (P + np.arange(P))[:, None] - np.arange(S)[None, :]
    masks = np.zeros((P, GROUPS, S), np.float32)
    for g, (window, dilation) in enumerate(WINDOWS):
        ok = (dist >= 0) & (dist <= window) & (dist % dilation == 0)
        masks[:, g, :] = np.where(ok, 0.0, NEG)

    feeds = {
        "stream": stream,
        "x_in": np.ascontiguousarray(arr("x").reshape(NT, P, D).transpose(1, 0, 2)),
        "small": small,
        "blockdiag": blockdiag.reshape(LAYERS, P, 2048),
        "norm_rows": norm_rows,
        "tables": tables,
        "masks": masks.reshape(P, GROUPS * S),
    }
    nc = bacc.Bacc("TRN2", target_bir_lowering=False, num_devices=1)
    aps = [nc.dram_tensor(n, a.shape, mybir.dt.float32, kind="ExternalInput").ap() for n, a in feeds.items()]
    o = nc.dram_tensor("out", (P, NT, D), mybir.dt.float32, kind="ExternalOutput").ap()
    build(nc, *aps, o)
    r = run(nc, [feeds], core_ids=[0])
    return np.ascontiguousarray(r.results[0]["out"].transpose(1, 0, 2)).reshape(1, S, D)
```

```python
import math
from contextlib import ExitStack

import numpy as np

import concourse.bass as bass
from concourse import mybir

P = 128
D = 1024
S = 256
NT = S // P
KD = D // P
LAYERS = 2
GROUPS = 3
HEADS = 8
HD = 64
WINDOWS = ((128, 1), (512, 4), (2048, 16))
NE = 16
EG = 4
EPS = 1e-6
CAP = 64
MORE = S // CAP - 1
NEG = -1.0e30

UCOL = 4 * 512
W_UNITS = 44
E_UNITS = 6
M_UNITS = NE * E_UNITS
UNITS = W_UNITS + M_UNITS
SLOTS = 3
RAW = 6
KEPT = 3
CREDIT = 2 * RAW
RAW_SLOT = [u % SLOTS if u < W_UNITS else (u - W_UNITS) % RAW for u in range(UNITS)]
for j in range(KEPT):
    RAW_SLOT[UNITS - E_UNITS + j] = RAW + j
RAW_USES = [RAW_SLOT.count(s) for s in range(RAW + KEPT)]
RAW_BEFORE = [RAW_SLOT[:W_UNITS].count(s) for s in range(RAW)]
POOL_AT = 1280

GROUP_KINDS = (["u"] * 2 + ["q"] * 3 + ["k"] * 3 + ["v"] * 3 + ["g"] * 2 + ["m"] * 4 + ["pl"] * 2
               + ["pa"] * 2 + ["wo"] * 2)
GROUP_UNITS = [1 if kind == "pa" else 2 for kind in GROUP_KINDS]
GROUP_START = [sum(GROUP_UNITS[:i]) for i in range(len(GROUP_KINDS))]
GROUP_END = {GROUP_START[i] + GROUP_UNITS[i]: i for i in range(len(GROUP_KINDS))}
NG = len(GROUP_KINDS)
PAIR_READS = [len(range(b, NG - 2, 2)) for b in range(2)]
G_STEPS = {end: n for n, end in enumerate(e for e, i in GROUP_END.items() if GROUP_KINDS[i] == "g")}
PA_STEPS = [end for end, i in GROUP_END.items() if GROUP_KINDS[i] == "pa"]
ATT0 = 11

C_N1, C_BA, C_BX, C_LAM, C_CB, C_CW, C_BM = 0, 8, 16, 24, 32, 40, 72
C_RW, C_RB, C_N2, SMALL = 88, 248, 268, 276


def turn(u):
    if u >= SLOTS:
        return u + 1
    last = max(v for v in range(UNITS) if v % SLOTS == u)
    return last - UNITS + 1 + SLOTS


def raw_turn(u):
    before = [v for v in range(u) if RAW_SLOT[v] == RAW_SLOT[u]]
    last = before[-1] if before else max(v for v in range(UNITS) if RAW_SLOT[v] == RAW_SLOT[u]) - UNITS
    return last + 1 + CREDIT


class Chain:

    def __init__(self, eng, sem):
        self.eng, self.sem, self.base, self.n = eng, sem, 0, 0

    def at(self, base):
        self.base, self.n = base, 0

    def step(self, ins):
        self.n += 1
        ins.then_inc(self.sem, 1)

    def join(self):
        self.eng.wait_ge(self.sem, self.base + self.n)

    def link(self, ins):
        self.step(ins)
        self.join()


DVE_LINKS = 123


def build(nc, stream, x, small, blockdiag, norm_rows, tables, masks, out):
    f32, f32r, bf16, i32, u32 = (mybir.dt.float32, mybir.dt.float32r, mybir.dt.bfloat16, mybir.dt.int32,
                                 mybir.dt.uint32)
    ALU, ACT, AX = mybir.AluOpType, mybir.ActivationFunctionType, mybir.AxisListType
    ds = bass.ds
    ctx = ExitStack()
    with ctx:
        def sb(name, shape, dt=f32):
            return ctx.enter_context(nc.sbuf_tensor(name, shape, dt))

        def sem(name):
            return ctx.enter_context(nc.semaphore(name))

        raws = sb("raws", [P, RAW, UCOL])
        high = sb("high", [P, SLOTS, UCOL], f32r)
        low = sb("low", [P, SLOTS, UCOL], f32r)
        xs = sb("xs", [P, NT, D])
        act_h = sb("act_h", [P, 2048], f32r)
        act_l = sb("act_l", [P, 2048], f32r)
        lru_h = sb("lru_h", [P, 2048], f32r)
        lru_l = sb("lru_l", [P, 2048], f32r)
        att_h = sb("att_h", [P, 1024], f32r)
        att_l = sb("att_l", [P, 1024], f32r)
        qk = raws[:, SLOTS:RAW, :].rearrange("p s n -> p (s n)")
        qT = qk[:, 0:12 * S].rearrange("p (c n) -> p c n", c=12)
        kT = qk[:, 12 * S:24 * S].rearrange("p (c n) -> p c n", c=12)
        v = sb("v", [P, NT, GROUPS * 512])
        s0 = sb("s0", [P, 8 * 259])
        s1 = sb("s1", [P, 2048])
        s2 = sb("s2", [P, 2048])
        s3 = sb("s3", [P, 2048])
        at = sb("at", [P, 2176])
        mask = sb("mask", [P, GROUPS, S], bf16)
        ident = sb("ident", [P, P])
        ident2 = sb("ident2", [P, CAP])
        tri, ones = sb("tri", [P, P], f32r), sb("ones", [P, P], f32r)
        iota = sb("iota", [P, 2 * CAP])
        cos2, sin2 = sb("cos2", [P, NT, HD]), sb("sin2", [P, NT, HD])
        smalls = sb("smalls", [P, LAYERS, SMALL])
        cur = sb("cur", [P, SMALL])
        sp = sb("sp", [P, 8, 8])
        ss_half = sb("ss_half", [P, 2, NT])
        ss, rstd, mhalf = sb("ss", [P, NT]), sb("rstd", [P, NT]), sb("mhalf", [P, NT])
        nmax, den, rden = sb("nmax", [P, NT]), sb("den", [P, NT]), sb("rden", [P, NT])
        lg = sb("lg", [P, NT, 20])
        g8, e8 = sb("g8", [P, NT, 8]), sb("e8", [P, NT, 8])
        gm, em = sb("gm", [P, NT, 8]), sb("em", [P, NT, 8])
        gi, ei = sb("gi", [P, NT, 8], u32), sb("ei", [P, NT, 8], u32)
        gf, ef = sb("gf", [P, NT, 8]), sb("ef", [P, NT, 8])
        goh, oh, oh_sum = sb("goh", [P, NT, EG]), sb("oh", [P, 2, NT, EG]), sb("oh_sum", [P, NT, EG])
        r16 = sb("r16", [P, NT, NE])
        rs = sb("rs", [P, 12, NT])
        sel, comb, rank = sb("sel", [P, NT, NE], f32r), sb("comb", [P, NT, NE]), sb("rank", [P, NT, NE + 1])
        over = sb("over", [P, 1])
        flag = sb("flag", [P, 1], i32)
        ws = sb("ws", [P, 1])

        xn = s0[:, 0:2048].rearrange("p (t d) -> p t d", t=NT)
        kept = [v[:, :, :].rearrange("p t n -> p (t n)")[:, D:D + UCOL], at[:, 0:UCOL], s3[:, :]]
        junk = s3[:, :].rearrange("p (t d) -> p t d", t=NT)
        upad = s0[:, :].rearrange("p (c n) -> p c n", c=8)
        conv = s1[:, :].rearrange("p (c n) -> p c n", c=8)
        rg, ig = s2[:, :].rearrange("p (c n) -> p c n", c=8), s3[:, :].rearrange("p (c n) -> p c n", c=8)
        decay = s0[:, 0:2048].rearrange("p (c n) -> p c n", c=8)
        rec = s1
        probs = s3[:, 0:1152]
        bd = at[:, 0:2048].rearrange("p (w c n) -> p w c n", w=2, c=8)
        pT = at[:, 0:1152]
        attn = at[:, 1152:2176].rearrange("p (t n) -> p t n", t=NT)
        nrow = v[:, 0, 0:D]
        h2 = xn
        x2T = s2[:, :].rearrange("p (c n) -> p c n", c=8)
        g_swapped = s2[:, 0:512]
        g_sum, tgate, act = (s1[:, n * 512:(n + 1) * 512] for n in range(3))
        hT_h, hT_l = (a[:, :].rearrange("p (c n) -> p c n", c=8) for a in (act_h, act_l))
        h2_h, h2_l = (a[:, :].rearrange("p (t d) -> p t d", t=NT) for a in (act_h, act_l))
        lT_h, lT_l = (a[:, :].rearrange("p (c n) -> p c n", c=8) for a in (lru_h, lru_l))
        aT_h, aT_l = (a[:, :].rearrange("p (c n) -> p c n", c=4) for a in (att_h, att_l))
        he = lru_h[:, 0:1024].rearrange("p (c n) -> p c n", c=8)
        y_h, y_l = lru_h[:, 1024:2048], lru_l[:, 1024:2048]
        ae = att_h[:, 0:512].rearrange("p (c n) -> p c n", c=4)
        pe_01 = att_h[:, 512:768].rearrange("p (t n) -> p t n", t=NT)
        pt_01 = att_h[:, 768:1024]

        pair = [ctx.enter_context(nc.psum_tensor(f"pair{b}", [P, 1024], f32)) for b in range(2)]
        pS = ctx.enter_context(nc.psum_tensor("pS", [P, 1536], f32))
        pO = ctx.enter_context(nc.psum_tensor("pO", [P, 512], f32))
        logits = [pO[:, 0:20], pS[:, 1024:1044]]
        bank = [pS[:, 0:512], pS[:, 512:1024], pS[:, 1024:1536], pO[:, :]]

        def raw(slot):
            return raws[:, slot, :] if slot < RAW else kept[slot - RAW]

        class Flow:

            def __init__(self, tag, units, first):
                self.units, self.first = units, first
                self.raw_uses = RAW_USES if first else [NE] * RAW
                self.raw_before = RAW_BEFORE if first else [0] * RAW
                self.raw_in = [sem(f"{tag}_raw_in{s}") for s in range(RAW + KEPT if first else RAW)]
                self.high_ready = sem(f"{tag}_high_ready")
                self.low_dve = sem(f"{tag}_low_dve")
                self.low_pool = sem(f"{tag}_low_pool")
                self.unit_used = sem(f"{tag}_unit_used")
                self.p_ready = sem(f"{tag}_p_ready")
                self.pt_done = sem(f"{tag}_pt_done")
                self.pt_ready = sem(f"{tag}_pt_ready")
                self.ws_ready = sem(f"{tag}_ws_ready")
                self.he_done0 = sem(f"{tag}_he_done0")
                self.he_done1 = sem(f"{tag}_he_done1")
                self.he_high0 = sem(f"{tag}_he_high0")
                self.he_high1 = sem(f"{tag}_he_high1")
                self.he_low0 = sem(f"{tag}_he_low0")
                self.he_low1 = sem(f"{tag}_he_low1")
                self.g_swapped = sem(f"{tag}_g_swapped")
                self.g_sum = sem(f"{tag}_g_sum")
                self.tanh_ready = sem(f"{tag}_tanh_ready")
                self.act_ready = sem(f"{tag}_act_ready")
                self.aeT_done = sem(f"{tag}_aeT_done")
                self.ae_high = sem(f"{tag}_ae_high")
                self.ae_low = sem(f"{tag}_ae_low")
                self.y_high0 = sem(f"{tag}_y_high0")
                self.y_high1 = sem(f"{tag}_y_high1")
                self.y_low0 = sem(f"{tag}_y_low0")
                self.y_low1 = sem(f"{tag}_y_low1")
                self.y_zero = sem(f"{tag}_y_zero")
                self.moe_done = sem(f"{tag}_moe_done")
                self.x_added = sem(f"{tag}_x_added")
                self.dve_chain = sem(f"{tag}_dve_chain")

        main, over_flow = Flow("m", UNITS, W_UNITS), Flow("o", M_UNITS, 0)
        (const_in, x_in, bd_in, nrow_in, out_done) = (sem(n) for n in (
            "const_in", "x_in", "bd_in", "nrow_in", "out_done"))
        (ss_ready, rstd_ready, xn_ready, xT_done, hT_high, hT_low, pair_read0, pair_read1) = (sem(n) for n in (
             "ss_ready", "rstd_ready", "xn_ready", "xT_done", "hT_high", "hT_low", "pair_read0",
             "pair_read1"))
        pair_read = [pair_read0, pair_read1]
        (cur_ready, pad_zero, u_ready, conv_ready, gate_mm, r_ready, i_ready, sp_ready,
         elam_ready, decay_ready, t_ready, v_ready, root_ready, rec_ready) = (sem(n) for n in (
             "cur_ready", "pad_zero", "u_ready", "conv_ready", "gate_mm", "r_ready",
             "i_ready", "sp_ready", "elam_ready", "decay_ready", "t_ready", "v_ready", "root_ready",
             "rec_ready"))
        (rot_ready, rotT_done, qkT_ready, g_ready, g_inner, g_tanh, lru_full, lT_high, lT_low) = (sem(n) for n in (
             "rot_ready", "rotT_done", "qkT_ready", "g_ready", "g_inner", "g_tanh", "lru_full",
             "lT_high", "lT_low"))
        (qk_done, max_ready, exp_ready, pT_done, pT_ready, pv_done, attn_ready, aT_done, aT_high, aT_low,
         mix_full, mix_high, mix_low, x_done) = (sem(n) for n in (
             "qk_done", "max_ready", "exp_ready", "pT_done", "pT_ready", "pv_done", "attn_ready", "aT_done",
             "aT_high", "aT_low", "mix_full", "mix_high", "mix_low", "x_done"))
        (h2_ready, h2_high, h2_low, x_mixed, x2T_done, x2T_ready, rw_ready, logits_done, gneg_ready, gexp_ready,
         diff_ready, e2_ready, sel_ready, comb_ready, rank_done, flag_ready, table_zero, ss_half_ready) = (
             sem(n) for n in (
                 "h2_ready", "h2_high", "h2_low", "x_mixed", "x2T_done", "x2T_ready", "rw_ready", "logits_done",
                 "gneg_ready", "gexp_ready", "diff_ready", "e2_ready", "sel_ready", "comb_ready", "rank_done",
                 "flag_ready", "table_zero", "ss_half_ready"))
        dve_chain, pool_chain, mask_in, wait_carried, rank_moved = (sem(n) for n in (
            "dve_chain", "pool_chain", "mask_in", "wait_carried", "rank_moved"))

        block = ctx.enter_context(nc.Block())

        def settled(eng):
            eng.sem_inc(wait_carried, 1)

        def gathered(half):
            return bank[2 + half].rearrange("p (c n) -> p c n", c=4)[:, :, 0:CAP]

        @block.sync
        def _(sp_eng):
            eng = sp_eng
            eng.dma_start(xs[:, :, :], x).then_inc(x_in, 16)
            eng.dma_start(smalls[:, :, :], small).then_inc(const_in, 16)
            eng.dma_start(ident[:, :], tables[:, 0:128]).then_inc(const_in, 16)
            eng.dma_start(s1[:, 0:P], tables[:, 128:256]).then_inc(const_in, 16)
            eng.dma_start(iota[:, :], tables[:, 256:384]).then_inc(const_in, 16)
            eng.dma_start(ident2[:, :], tables[:, 384:384 + CAP]).then_inc(const_in, 16)
            eng.dma_start(cos2[:, :, :], tables[:, 512:640].rearrange("p (t n) -> p t n", t=NT)
                          ).then_inc(const_in, 16)
            eng.dma_start(sin2[:, :, :], tables[:, 640:768].rearrange("p (t n) -> p t n", t=NT)
                          ).then_inc(const_in, 16)
            eng.dma_start(s2[:, 0:768], masks).then_inc(mask_in, 16)

            def load(flow, slot, after, unit_row):
                eng.wait_ge(flow.low_dve, after)
                eng.wait_ge(flow.low_pool, after)
                eng.dma_start(raw(slot), stream[ds(unit_row, 1), :, :].rearrange("o p n -> (o p) n")
                              ).then_inc(flow.raw_in[slot], 16)

            def load_expert(flow, l, e, first, row, begin=0):
                for j in range(begin, E_UNITS):
                    load(flow, j, l * flow.units + e * E_UNITS + (first + j + 1 - E_UNITS + CREDIT), row + j)

            with eng.Fori(0, LAYERS) as l:
                for u in range(W_UNITS + RAW):
                    if u == W_UNITS + SLOTS:
                        eng.wait_ge(qk_done, l * 8 + 8)
                    load(main, RAW_SLOT[u], l * UNITS + raw_turn(u), l * UNITS + u)
                for slot, done, count in ((RAW, pv_done, 8), (RAW + 1, aT_done, 2), (RAW + 2, ss_half_ready, 4)):
                    eng.wait_ge(done, (l + 1) * count)
                    eng.dma_start(raw(slot), stream[ds(l * UNITS + RAW_SLOT.index(slot), 1), :, :]
                                  .rearrange("o p n -> (o p) n")).then_inc(main.raw_in[slot], 16)
                with eng.Fori(1, NE - 1) as e:
                    load_expert(main, l, e, W_UNITS, l * UNITS + e * E_UNITS + W_UNITS)
                load_expert(main, l, NE - 1, W_UNITS, l * UNITS + (UNITS - E_UNITS), KEPT)
                eng.wait_ge(flag_ready, l + 1)
                settled(eng)
                more = eng.value_load(flag[0:1, 0:1], min_val=0, max_val=1)
                with eng.If(more > 0):
                    eng.wait_ge(main.low_dve, l * UNITS + UNITS + CREDIT)
                    eng.wait_ge(main.low_pool, l * UNITS + UNITS + CREDIT)
                    settled(eng)
                    with eng.Fori(0, MORE) as q:
                        with eng.Fori(0, NE) as e:
                            load_expert(over_flow, l * MORE + q, e, 0, l * UNITS + e * E_UNITS + W_UNITS)
                    eng.wait_ge(over_flow.low_dve, (l + 1) * (MORE * M_UNITS) + CREDIT)
                    eng.wait_ge(over_flow.low_pool, (l + 1) * (MORE * M_UNITS) + CREDIT)
                    settled(eng)
                with eng.Else():
                    for s in range(RAW):
                        eng.sem_inc(over_flow.raw_in[s], 16 * NE * MORE)
            for t in range(NT):
                eng.wait_ge(out_done, t + 1)
                eng.dma_start(out[:, t, :], xn[:, t, :]).then_inc(x_in, 16)
            eng.wait_ge(x_in, 16 * (1 + NT))

        @block.scalar
        def _(act_eng):
            eng = act_eng
            def split_high(flow, raw_slot, in_count, used_count, slot):
                eng.wait_ge(flow.raw_in[raw_slot], in_count)
                eng.wait_ge(flow.unit_used, used_count)
                nc.scalar.activation(high[:, slot, :], raw(raw_slot), ACT.Copy).then_inc(flow.high_ready, 1)

            def split_w(l, u):
                s = RAW_SLOT[u]
                split_high(main, s, (l * RAW_USES[s] + RAW_SLOT[:u + 1].count(s)) * 16, l * UNITS + turn(u),
                           u % SLOTS)

            def sum_squares(tiles_before):
                for t in range(NT):
                    eng.wait_ge(x_done, tiles_before + t + 1)
                    nc.scalar.activation(junk[:, t, :], xs[:, t, :], ACT.Square,
                                         accum_out=ss[:, t:t + 1]).then_inc(ss_ready, 1)

            def load_row(row):
                eng.dma_start(nrow, norm_rows[ds(row, 1), :, :].rearrange("o p n -> (o p) n")
                              ).then_inc(nrow_in, 16)

            def moe(flow, l, first):
                def split(e, j, to_end):
                    used = l * flow.units + e * E_UNITS + (first + j + 1)
                    if first and to_end == 0 and j < KEPT:
                        split_high(flow, RAW + j, (l + 1) * 16, used, (first + j) % SLOTS)
                    else:
                        split_high(flow, j, (l * flow.raw_uses[j] + e + (flow.raw_before[j] + 1)) * 16, used,
                                   (first + j) % SLOTS)

                def evac_he(e_next, half):
                    eng.wait_ge([flow.he_done0, flow.he_done1][half], l * (NE + 1) + e_next + 1)
                    nc.scalar.activation(he[:, 4 * half:4 * half + 4, 0:CAP],
                                         gathered(half), ACT.Copy
                                         ).then_inc([flow.he_high0, flow.he_high1][half], 1)

                def expert(e, to_end):
                    split(e, 2, to_end)
                    split(e, 3, to_end)
                    eng.wait_ge(flow.unit_used, l * flow.units + e * E_UNITS + (first + 2 + SLOTS))
                    nc.scalar.activation(g_swapped[0:CAP, :], bank[0][CAP:P, :], ACT.Copy)
                    nc.scalar.activation(g_swapped[CAP:P, :], bank[0][0:CAP, :], ACT.Copy
                                         ).then_inc(flow.g_swapped, 1)
                    eng.wait_ge(flow.pt_done, l * NE + e + 1)
                    nc.scalar.activation(pt_01, bank[2][:, 0:S], ACT.Copy).then_inc(flow.pt_ready, 1)
                    eng.wait_ge(flow.g_sum, l * NE + e + 1)
                    nc.scalar.activation(tgate, g_sum, ACT.Tanh, scale=0.5).then_inc(flow.tanh_ready, 1)
                    split(e, 4, to_end)
                    split(e, 5, to_end)
                    evac_he(e + 1, 0)
                    eng.wait_ge(flow.aeT_done, l * NE + e + 1)
                    nc.scalar.activation(ae[:, :, 0:CAP], bank[0][:, 0:256].rearrange("p (c n) -> p c n", c=4),
                                         ACT.Copy
                                         ).then_inc(flow.ae_high, 1)
                    if to_end:
                        split(e + 1, 0, to_end - 1)
                    evac_he(e + 1, 1)
                    for half in range(2):
                        if half and to_end:
                            split(e + 1, 1, to_end - 1)
                        eng.wait_ge(flow.unit_used, l * flow.units + e * E_UNITS + (first + 5 + half + SLOTS))
                        eng.wait_ge(flow.ws_ready, l * NE + e + 1)
                        nc.scalar.activation(y_h[:, 512 * half:512 * half + 512], bank[1 + half], ACT.Copy,
                                             scale=ws[:, 0:1]).then_inc([flow.y_high0, flow.y_high1][half], 1)

                evac_he(0, 0)
                evac_he(0, 1)
                with eng.Fori(0, NE - 2) as e:
                    expert(e, 2)
                expert(NE - 2, 1)
                expert(NE - 1, 0)

            for flow in (main, over_flow):
                eng.sem_inc(flow.y_high0, 1)
                eng.sem_inc(flow.y_high1, 1)
            eng.wait_ge(x_in, 16)
            with eng.Fori(0, LAYERS) as l:
                sum_squares(l * 2)
                split_w(l, 0)
                eng.wait_ge(cur_ready, l * 2 + 2)
                for c in range(8):
                    if c % 2 == 0:
                        eng.wait_ge(xT_done, l * 4 + c // 2 + 1)
                    nc.scalar.activation(hT_h[:, c, :], pair[c // 4][:, (c % 4) * S:(c % 4 + 1) * S], ACT.Copy,
                                         scale=cur[:, C_N1 + c:C_N1 + c + 1]).then_inc(hT_high, 1)
                eng.dma_start(at[:, 0:2048], blockdiag[ds(l, 1), :, :].rearrange("o p n -> (o p) n")
                              ).then_inc(bd_in, 16)
                split_w(l, 1)
                split_w(l, 2)
                eng.wait_ge(elam_ready, l * 2 + 1)
                nc.scalar.activation(sp[:, 2, :], sp[:, 1, :], ACT.Exp, scale=-1.0).then_inc(elam_ready, 1)

                for u in range(3, W_UNITS + 1):
                    if u - 2 not in PA_STEPS:
                        split_w(l, u)
                    for p in ([u - 1] if u < W_UNITS else [W_UNITS - 1, W_UNITS]):
                        i = GROUP_END.get(p)
                        kind = GROUP_KINDS[i] if i is not None else None
                        b = None if i is None else i % 2
                        done = None if i is None else l * UNITS + (p + SLOTS)
                        if kind == "u":
                            c0 = 4 * i
                            eng.wait_ge(main.unit_used, done)
                            eng.wait_ge(pad_zero, l + 1)
                            nc.scalar.activation(upad[:, c0:c0 + 4, 3:3 + S],
                                                 pair[b][:, :].rearrange("p (c n) -> p c n", c=4), ACT.Copy
                                                 ).then_inc(u_ready, 1)
                            for c in range(4):
                                ins = nc.scalar.activation(conv[:, c0 + c, :], pair[b][:, c * S:(c + 1) * S],
                                                           ACT.Identity,
                                                           scale=cur[:, C_CW + 24 + c0 + c:C_CW + 25 + c0 + c],
                                                           bias=cur[:, C_CB + c0 + c:C_CB + c0 + c + 1])
                            ins.then_inc(pair_read[b], 1)
                        if kind == "v":
                            eng.wait_ge(main.unit_used, done)
                            g = i - 8
                            nc.scalar.activation(v[:, :, g * 512:(g + 1) * 512],
                                                 pair[b][:, :].rearrange("p (t n) -> p t n", t=NT), ACT.Copy
                                                 ).then_inc(pair_read[b], 1)
                        if 5 <= p <= 8:
                            for c in range(2 * (p - 5), 2 * (p - 5) + 2):
                                eng.wait_ge(gate_mm, l * 8 + c + 1)
                                ps = pS[:, (c % 3) * 512:(c % 3) * 512 + 512]
                                nc.scalar.activation(rg[:, c, :], ps[:, 0:S], ACT.Tanh, scale=0.5,
                                                     bias=cur[:, C_BA + c:C_BA + c + 1]).then_inc(r_ready, 1)
                                nc.scalar.activation(ig[:, c, :], ps[:, S:2 * S], ACT.Tanh, scale=0.5,
                                                     bias=cur[:, C_BX + c:C_BX + c + 1]).then_inc(i_ready, 1)
                        if p == 9:
                            eng.wait_ge(sp_ready, l * 2 + 2)
                            eng.wait_ge(conv_ready, l * 8 + 8)
                            eng.wait_ge(r_ready, l * 8 + 8)
                            for c in range(8):
                                nc.scalar.activation(decay[:, c, :], rg[:, c, :], ACT.Exp,
                                                     scale=sp[:, 6, c:c + 1], bias=sp[:, 6, c:c + 1]
                                                     ).then_inc(decay_ready, 1)
                                nc.scalar.activation(rg[:, c, :], rg[:, c, :], ACT.Tanh,
                                                     scale=sp[:, 7, c:c + 1], bias=sp[:, 7, c:c + 1]
                                                     ).then_inc(t_ready, 1)
                        if p == 12:
                            eng.wait_ge(v_ready, l + 1)
                            nc.scalar.activation(s2[:, :], s2[:, :], ACT.Sqrt, scale=0.25).then_inc(root_ready, 1)
                        for tile in range(NT):
                            j = GROUP_END.get(p - 1 - tile)
                            if j is not None and GROUP_KINDS[j] in "qk":
                                n = (j - 2) * NT + tile
                                eng.wait_ge(rotT_done, l * 12 + n + 1)
                                dst = qT if GROUP_KINDS[j] == "q" else kT
                                g = (j - 2) % 3
                                nc.scalar.activation(dst[:, 4 * g:4 * g + 4, tile * P:(tile + 1) * P],
                                                     pO[:, :].rearrange("p (c n) -> p c n", c=4), ACT.Copy
                                                     ).then_inc(qkT_ready, 1)
                        half = G_STEPS.get(p - 2)
                        if half is not None:
                            eng.wait_ge(lru_full, l * 2 + half + 1)
                            nc.scalar.activation(lru_h[:, half * 1024:half * 1024 + 1024],
                                                 s2[:, half * 1024:half * 1024 + 1024], ACT.Copy
                                                 ).then_inc(lT_high, 1)
                        if 2 * ATT0 <= p < 2 * (ATT0 + HEADS) and p % 2 == 0:
                            h = p // 2 - ATT0
                            for t in range(NT):
                                eng.wait_ge(max_ready, l * 16 + 2 * h + t + 1)
                                pr = probs[:, 0:768] if t == 1 else probs[:, 768:1152]
                                nc.scalar.activation(pr, pr, ACT.Exp, bias=nmax[:, t:t + 1],
                                                     accum_out=den[:, t:t + 1]).then_inc(exp_ready, 1)
                        if 2 * ATT0 < p < 2 * (ATT0 + HEADS) and p % 2 == 1:
                            h = p // 2 - ATT0
                            eng.wait_ge(pT_done, l * 8 + h + 1)
                            nc.scalar.activation(pT, pS[:, 0:1152], ACT.Copy).then_inc(pT_ready, 1)
                        if kind == "m":
                            n = i - 13
                            eng.wait_ge(main.unit_used, done)
                            eng.wait_ge(lT_low, l * 2 + 2)
                            dst = s2 if n < 2 else s0
                            for c in range(4):
                                cc = 4 * (n % 2) + c
                                bm = C_BM + (8 if n < 2 else 0) + cc
                                ins = nc.scalar.activation(dst[:, cc * S:(cc + 1) * S],
                                                           pair[b][:, c * S:(c + 1) * S], ACT.Tanh, scale=0.5,
                                                           bias=cur[:, bm:bm + 1])
                            ins.then_inc(pair_read[b], 1)
                        if p in G_STEPS:
                            half = G_STEPS[p]
                            eng.wait_ge(main.unit_used, done)
                            eng.wait_ge(rec_ready, l * 8 + 8)
                            nc.scalar.activation(s2[:, half * 1024:half * 1024 + 1024], pair[b][:, :], ACT.Square
                                                 ).then_inc(g_ready, 1)
                            nc.scalar.activation(s0[:, half * 1024:half * 1024 + 1024], pair[b][:, :], ACT.Copy
                                                 ).then_inc(pair_read[b], 1)
                        half = G_STEPS.get(p - 1)
                        if half is not None:
                            eng.wait_ge(g_inner, l * 2 + half + 1)
                            nc.scalar.activation(s2[:, half * 1024:half * 1024 + 1024],
                                                 s2[:, half * 1024:half * 1024 + 1024], ACT.Tanh,
                                                 scale=math.sqrt(2.0 / math.pi)).then_inc(g_tanh, 1)
                        if p == 38:
                            eng.wait_ge(pv_done, l * 8 + 8)
                            load_row(l)
                            for n in range(2):
                                eng.wait_ge(aT_done, l * 2 + n + 1)
                                cols = slice(512 * n, 512 * n + 512)
                                nc.scalar.activation(att_h[:, cols], pS[:, cols], ACT.Copy).then_inc(aT_high, 1)
                        if kind == "pa":
                            half = i - 19
                            split_w(l, p + 2)
                            eng.wait_ge(mix_full, l * 2 + half + 1)
                            nc.scalar.activation(act_h[:, half * 1024:half * 1024 + 1024],
                                                 s0[:, half * 1024:half * 1024 + 1024], ACT.Copy, scale=0.5
                                                 ).then_inc(mix_high, 1)
                        if p == W_UNITS - 2:
                            eng.wait_ge(x_mixed, l * 3 + 1)
                            for t in range(NT):
                                nc.scalar.activation(junk[:, t, 0:512], xs[:, t, 0:512], ACT.Square,
                                                     accum_out=ss_half[:, 0, t:t + 1]).then_inc(ss_half_ready, 1)
                        if p == W_UNITS - 1:
                            for n in range(2):
                                eng.wait_ge(x2T_done, l * 4 + n + 1)
                                nc.scalar.activation(s2[:, 512 * n:512 * n + 512],
                                                     pair[1][:, 512 * n:512 * n + 512], ACT.Copy
                                                     ).then_inc(x2T_ready, 1)
                            split_w(l, W_UNITS + 1)
                for t in range(NT):
                    eng.wait_ge(x_mixed, l * 3 + t + 2)
                    nc.scalar.activation(junk[:, t, 512:D], xs[:, t, 512:D], ACT.Square,
                                         accum_out=ss_half[:, 1, t:t + 1]).then_inc(ss_half_ready, 1)
                for n in range(2):
                    eng.wait_ge(x2T_done, l * 4 + n + 3)
                    nc.scalar.activation(s2[:, 1024 + 512 * n:1536 + 512 * n], bank[n], ACT.Copy
                                         ).then_inc(x2T_ready, 1)
                for t in range(NT):
                    eng.wait_ge(h2_ready, l * 2 + t + 1)
                    nc.scalar.activation(h2_h[:, t, :], h2[:, t, :], ACT.Copy).then_inc(h2_high, 1)
                for t in range(NT):
                    eng.wait_ge(gneg_ready, l + 1)
                    nc.scalar.activation(rs[:, 6 + 2 * t:8 + 2 * t, :].rearrange("p a b -> p (a b)"),
                                         lg[:, t, 0:EG], ACT.Exp, bias=rs[:, 0, t:t + 1],
                                         accum_out=rs[:, 1, t:t + 1]).then_inc(gexp_ready, 1)
                eng.wait_ge(diff_ready, l + 1)
                nc.scalar.activation(rs[:, 3, :], rs[:, 2, :], ACT.Exp).then_inc(e2_ready, 1)
                eng.wait_ge(flag_ready, l + 1)
                settled(eng)
                more = eng.value_load(flag[0:1, 0:1], min_val=0, max_val=1)
                moe(main, l, W_UNITS)
                with eng.If(more > 0):
                    eng.wait_ge(main.unit_used, l * UNITS + UNITS + SLOTS)
                    with eng.Fori(0, MORE) as q:
                        n = l * MORE + q
                        for j in range(2):
                            split_high(over_flow, j, (n * NE + 1) * 16, n * M_UNITS + j + 1, j)
                        moe(over_flow, n, 0)
                    eng.wait_ge(over_flow.unit_used, (l + 1) * (MORE * M_UNITS) + SLOTS)
                    settled(eng)
                with eng.Else():
                    eng.sem_inc(over_flow.high_ready, M_UNITS * MORE)
                    for sm, k in ((over_flow.pt_ready, NE), (over_flow.he_high0, NE + 1),
                                  (over_flow.he_high1, NE + 1), (over_flow.tanh_ready, NE),
                                  (over_flow.g_swapped, NE),
                                  (over_flow.ae_high, NE), (over_flow.y_high0, NE), (over_flow.y_high1, NE)):
                        eng.sem_inc(sm, k * MORE)
            sum_squares(LAYERS * 2)
            load_row(LAYERS)
            eng.wait_ge(nrow_in, 16 * (LAYERS + 1))

        @block.gpsimd
        def _(pool_eng):
            eng = pool_eng
            for flow in (main, over_flow):
                eng.sem_inc(flow.low_pool, CREDIT)
            nc.gpsimd.memset(mhalf[:, :], -0.5).then_inc(pool_chain, 1)

            def split_low(flow, count, raw_slot, slot):
                eng.wait_ge(flow.high_ready, count)
                nc.gpsimd.tensor_tensor(low[:, slot, POOL_AT:UCOL], raw(raw_slot)[:, POOL_AT:UCOL],
                                        high[:, slot, POOL_AT:UCOL].bitcast(f32), ALU.subtract
                                        ).then_inc(flow.low_pool, 1)

            def split_w(l, u):
                split_low(main, l * UNITS + u + 1, RAW_SLOT[u], u % SLOTS)

            def power(t, count):
                col = slice(t, t + 1)
                nc.gpsimd.tensor_scalar(rstd[:, col], ss[:, col], 1.0 / D, EPS, ALU.mult, ALU.add
                                        ).then_inc(pool_chain, 1)
                eng.wait_ge(pool_chain, count)
                nc.gpsimd.tensor_tensor(rstd[:, col], rstd[:, col], mhalf[:, col], ALU.pow
                                        ).then_inc(rstd_ready, 1)

            with eng.Fori(0, LAYERS) as l:
                for t in range(NT):
                    eng.wait_ge(ss_ready, l * 2 + t + 1)
                    settled(eng)
                    power(t, l * 6 + t + 2)
                for u in range(SLOTS):
                    split_w(l, u)
                eng.wait_ge(xT_done, l * 4 + 4)
                settled(eng)
                nc.gpsimd.memset(upad[:, :, 0:3], 0.0).then_inc(pad_zero, 1)
                for u in range(SLOTS, W_UNITS + 2):
                    split_w(l, u)
                for t in range(NT):
                    eng.wait_ge(ss_half_ready, l * 4 + t + 3)
                    nc.gpsimd.tensor_tensor(ss[:, t:t + 1], ss_half[:, 0, t:t + 1], ss_half[:, 1, t:t + 1], ALU.add
                                            ).then_inc(pool_chain, 1)
                    eng.wait_ge(pool_chain, l * 6 + 2 * t + 4)
                    settled(eng)
                    power(t, l * 6 + 2 * t + 5)
                for t in range(NT):
                    eng.wait_ge(h2_high, l * 2 + t + 1)
                    nc.gpsimd.tensor_tensor(h2_l[:, t, :], h2[:, t, :], h2_h[:, t, :].bitcast(f32), ALU.subtract
                                            ).then_inc(h2_low, 1)
                with eng.Fori(0, NE - 2) as e:
                    for j in range(2, E_UNITS + 2):
                        split_low(main, l * UNITS + e * E_UNITS + (W_UNITS + j + 1), j % RAW,
                                  (W_UNITS + j) % SLOTS)
                for u in range(UNITS - 2 * E_UNITS + 2, UNITS):
                    split_w(l, u)
                eng.wait_ge(flag_ready, l + 1)
                settled(eng)
                more = eng.value_load(flag[0:1, 0:1], min_val=0, max_val=1)
                with eng.If(more > 0):
                    with eng.Fori(0, MORE * NE) as i:
                        for j in range(RAW):
                            split_low(over_flow, l * (MORE * M_UNITS) + i * RAW + (j + 1), j, j % SLOTS)
                with eng.Else():
                    eng.sem_inc(over_flow.low_pool, M_UNITS * MORE)
            for t in range(NT):
                eng.wait_ge(ss_ready, LAYERS * 2 + t + 1)
                power(t, LAYERS * 6 + t + 2)

        @block.vector
        def _(dve_eng):
            eng = dve_eng
            chain = Chain(eng, dve_chain)
            for flow in (main, over_flow):
                eng.sem_inc(flow.low_dve, CREDIT)
                eng.sem_inc(flow.y_low0, 1)
                eng.sem_inc(flow.y_low1, 1)
            eng.sem_inc(x_done, NT)

            def split_low(flow, count, raw_slot, slot):
                eng.wait_ge(flow.high_ready, count)
                nc.vector.tensor_tensor(low[:, slot, 0:POOL_AT], raw(raw_slot)[:, 0:POOL_AT],
                                        high[:, slot, 0:POOL_AT].bitcast(f32), ALU.subtract
                                        ).then_inc(flow.low_dve, 1)

            def split_w(l, u):
                split_low(main, l * UNITS + u + 1, RAW_SLOT[u], u % SLOTS)

            def slots_of(flow, e_col):
                for t in range(NT):
                    ins = nc.vector.tensor_scalar(pe_01[:, t, :], iota[:, :],
                                                  rank[:, t, ds(e_col, 1)], None, ALU.is_equal)
                ins.then_inc(flow.p_ready, 1)

            def y_zeros(flow):
                settled(eng)
                nc.vector.memset(y_h.bitcast(f32), 0.0)
                nc.vector.memset(y_l.bitcast(f32), 0.0).then_inc(flow.y_zero, 1)

            def add_experts(flow, l, added):
                for t in range(NT):
                    eng.wait_ge(flow.moe_done, l * NT + t + 1)
                    nc.vector.tensor_tensor(xs[:, t, :], xs[:, t, :], pair[t][:, :], ALU.add).then_inc(added, 1)

            def moe(flow, l, first):
                def split(e, j, to_end):
                    slot = RAW + j if first and to_end == 0 and j < KEPT else j
                    split_low(flow, l * flow.units + e * E_UNITS + (first + j + 1), slot, (first + j) % SLOTS)

                def low_he(e_next, half):
                    eng.wait_ge([flow.he_high0, flow.he_high1][half], l * (NE + 1) + e_next + 1)
                    c = slice(4 * half, 4 * half + 4)
                    nc.vector.tensor_tensor(he[:, c, CAP:P],
                                            gathered(half),
                                            he[:, c, 0:CAP].bitcast(f32), ALU.subtract
                                            ).then_inc([flow.he_low0, flow.he_low1][half], 1)

                def expert(e, to_end):
                    split(e, 2, to_end)
                    split(e, 3, to_end)
                    eng.wait_ge(flow.g_swapped, l * NE + e + 1)
                    nc.vector.tensor_tensor(g_sum, g_swapped, bank[0], ALU.add).then_inc(flow.g_sum, 1)
                    eng.wait_ge(flow.tanh_ready, l * NE + e + 1)
                    nc.vector.scalar_tensor_tensor(tgate, tgate, 1.0, g_sum, ALU.add, ALU.mult
                                                   ).then_inc(flow.dve_chain, 1)
                    eng.wait_ge(flow.pt_ready, l * NE + e + 1)
                    nc.vector.tensor_copy(ws[:, :], bank[2][:, S:S + 1]).then_inc(flow.ws_ready, 1)
                    slots_of(flow, e + 1)
                    eng.wait_ge(flow.dve_chain, l * NE + e + 1)
                    eng.wait_ge(flow.unit_used, l * flow.units + e * E_UNITS + (first + 4 + SLOTS))
                    nc.vector.scalar_tensor_tensor(act, tgate, 0.5, bank[1], ALU.mult, ALU.mult
                                                   ).then_inc(flow.act_ready, 1)
                    split(e, 4, to_end)
                    split(e, 5, to_end)
                    eng.wait_ge(flow.ae_high, l * NE + e + 1)
                    nc.vector.tensor_tensor(ae[:, :, CAP:P],
                                            bank[0][:, 0:256].rearrange("p (c n) -> p c n", c=4),
                                            ae[:, :, 0:CAP].bitcast(f32), ALU.subtract
                                            ).then_inc(flow.ae_low, 1)
                    low_he(e + 1, 0)
                    if to_end:
                        split(e + 1, 0, to_end - 1)
                    low_he(e + 1, 1)
                    for half in range(2):
                        eng.wait_ge([flow.y_high0, flow.y_high1][half], l * NE + e + 2)
                        eng.wait_ge(flow.ws_ready, l * NE + e + 1)
                        cols = slice(512 * half, 512 * half + 512)
                        nc.vector.scalar_tensor_tensor(y_l[:, cols], bank[1 + half], ws[:, 0:1],
                                                       y_h[:, cols].bitcast(f32), ALU.mult, ALU.subtract
                                                       ).then_inc([flow.y_low0, flow.y_low1][half], 1)
                        if half == 0 and to_end:
                            split(e + 1, 1, to_end - 1)

                low_he(0, 0)
                low_he(0, 1)
                with eng.Fori(0, NE - 2) as e:
                    expert(e, 2)
                expert(NE - 2, 1)
                expert(NE - 1, 0)

            nc.vector.memset(ones[:, :].bitcast(f32), 1.0).then_inc(table_zero, 1)
            nc.vector.memset(g8[:, :, :], -3.0e38).then_inc(table_zero, 1)
            nc.vector.memset(e8[:, :, :], -3.0e38).then_inc(table_zero, 1)
            nc.vector.memset(rank[:, :, :], -1.0).then_inc(table_zero, 1)
            nc.vector.memset(pt_01.bitcast(f32), 0.0).then_inc(table_zero, 1)
            eng.wait_ge(const_in, 112)
            nc.vector.tensor_copy(tri[:, :], s1[:, 0:P]).then_inc(table_zero, 1)
            eng.wait_ge(mask_in, 16)
            nc.vector.tensor_copy(mask[:, :, :], s2[:, 0:768].rearrange("p (g n) -> p g n", g=GROUPS)
                                  ).then_inc(table_zero, 1)
            eng.wait_ge(table_zero, 7)

            with eng.Fori(0, LAYERS) as l:
                chain.at(l * DVE_LINKS)
                chain.link(nc.vector.tensor_copy(cur[:, :], smalls[:, ds(l, 1), :].rearrange("p o n -> p (o n)")))
                nc.vector.tensor_scalar(cur[:, C_BA:C_BX + 8], cur[:, C_BA:C_BX + 8], 0.5, None, ALU.mult
                                        ).then_inc(cur_ready, 1)
                nc.vector.tensor_scalar(cur[:, C_BM:C_BM + 16], cur[:, C_BM:C_BM + 16], 0.5, None, ALU.mult
                                        ).then_inc(cur_ready, 1)
                rw = cur[:, C_RW:C_RW + 20 * KD].rearrange("p (k n) -> p k n", k=KD)
                nc.vector.tensor_tensor(rw, rw, cur[:, C_N2:C_N2 + KD].unsqueeze(2).to_broadcast([P, KD, 20]),
                                        ALU.mult).then_inc(rw_ready, 1)
                for t in range(NT):
                    eng.wait_ge(rstd_ready, l * 4 + t + 1)
                    nc.vector.tensor_scalar(xn[:, t, :], xs[:, t, :], rstd[:, t:t + 1], None, ALU.mult
                                            ).then_inc(xn_ready, 1)
                lam = cur[:, C_LAM:C_LAM + 8]
                chain.link(nc.vector.tensor_scalar(sp[:, 0, :], lam, -1.0, None, ALU.mult))
                nc.vector.tensor_tensor(sp[:, 1, :], lam, sp[:, 0, :], ALU.max).then_inc(elam_ready, 1)
                split_w(l, 0)
                for c in range(8):
                    if c % 2 == 0:
                        eng.wait_ge(hT_high, l * 8 + c + 2)
                    nc.vector.scalar_tensor_tensor(hT_l[:, c, :], pair[c // 4][:, (c % 4) * S:(c % 4 + 1) * S],
                                                   cur[:, C_N1 + c:C_N1 + c + 1],
                                                   hT_h[:, c, :].bitcast(f32), ALU.mult, ALU.subtract
                                                   ).then_inc(hT_low, 1)
                split_w(l, 1)
                split_w(l, 2)
                eng.wait_ge(elam_ready, l * 2 + 2)
                ee, s_, s2_, acc = sp[:, 2, :], sp[:, 3, :], sp[:, 4, :], sp[:, 5, :]
                chain.link(nc.vector.tensor_scalar(s_, ee, 2.0, None, ALU.add))
                chain.link(nc.vector.reciprocal(s_, s_))
                chain.link(nc.vector.tensor_tensor(s_, s_, ee, ALU.mult))
                chain.link(nc.vector.tensor_tensor(s2_, s_, s_, ALU.mult))
                chain.link(nc.vector.tensor_scalar(acc, s2_, 1.0 / 17.0, None, ALU.mult))
                for odd in (15, 13, 11, 9, 7, 5, 3):
                    chain.link(nc.vector.scalar_tensor_tensor(acc, acc, 1.0 / odd, s2_, ALU.add, ALU.mult))
                chain.link(nc.vector.scalar_tensor_tensor(acc, acc, 1.0, s_, ALU.add, ALU.mult))
                chain.link(nc.vector.tensor_scalar(sp[:, 0, :], sp[:, 0, :], 0.0, None, ALU.max))
                chain.link(nc.vector.scalar_tensor_tensor(acc, acc, 2.0, sp[:, 0, :], ALU.mult, ALU.add))
                nc.vector.tensor_scalar(sp[:, 6, :], acc, -4.0, None, ALU.mult).then_inc(sp_ready, 1)
                nc.vector.tensor_scalar(sp[:, 7, :], acc, 4.0, None, ALU.mult).then_inc(sp_ready, 1)

                for u in range(3, W_UNITS + 1):
                    if u - 2 not in PA_STEPS:
                        split_w(l, u)
                    for p in ([u - 1] if u < W_UNITS else [W_UNITS - 1, W_UNITS]):
                        i = GROUP_END.get(p)
                        kind = GROUP_KINDS[i] if i is not None else None
                        b = None if i is None else i % 2
                        done = None if i is None else l * UNITS + (p + SLOTS)
                        if kind == "u":
                            eng.wait_ge(u_ready, l * 2 + i + 1)
                            eng.wait_ge(pair_read[b], l * PAIR_READS[b] + (i // 2 + 1))
                            for tap in range(2, -1, -1):
                                for c in range(4 * i, 4 * i + 4):
                                    w = cur[:, C_CW + 8 * tap + c:C_CW + 8 * tap + c + 1]
                                    ins = nc.vector.scalar_tensor_tensor(conv[:, c, :], upad[:, c, tap:tap + S], w,
                                                                         conv[:, c, :], ALU.mult, ALU.add)
                                    if tap:
                                        ins.then_inc(dve_chain, 1)
                                        chain.n += 1
                                    else:
                                        ins.then_inc(conv_ready, 1)
                                if tap:
                                    eng.wait_ge(dve_chain, chain.base + chain.n)
                        if kind in ("q", "k"):
                            eng.wait_ge(main.unit_used, done)
                            for t in range(NT):
                                n = (i - 2) * NT + t
                                if n >= 2:
                                    eng.wait_ge(rotT_done, l * 12 + n - 1)
                                xq = pair[b][:, t * 512:(t + 1) * 512].rearrange("p (h n) -> p h n", h=HEADS)
                                a = v[:, 0, 512 + 512 * t:1024 + 512 * t].rearrange("p (h n) -> p h n", h=HEADS)
                                c_ = v[:, 1, 512 + 512 * t:1024 + 512 * t].rearrange("p (h n) -> p h n", h=HEADS)
                                cs = cos2[:, t, :].unsqueeze(1).to_broadcast([P, HEADS, HD])
                                sn = sin2[:, t, :].unsqueeze(1).to_broadcast([P, HEADS, HD])
                                nc.vector.tensor_tensor(a, xq, cs, ALU.mult).then_inc(dve_chain, 1)
                                nc.vector.tensor_tensor(c_[:, :, 0:32], xq[:, :, 32:64], sn[:, :, 0:32], ALU.mult
                                                        ).then_inc(dve_chain, 1)
                                nc.vector.tensor_tensor(c_[:, :, 32:64], xq[:, :, 0:32], sn[:, :, 32:64], ALU.mult
                                                        ).then_inc(pair_read[b] if t else dve_chain, 1)
                                chain.n += 2 if t else 3
                                eng.wait_ge(dve_chain, chain.base + chain.n)
                                if t:
                                    eng.wait_ge(pair_read[b], l * PAIR_READS[b] + (i // 2 + 1))
                                nc.vector.tensor_tensor(a, a, c_, ALU.add).then_inc(rot_ready, 1)
                        if p == 9:
                            eng.wait_ge(i_ready, l * 8 + 8)
                            eng.wait_ge(conv_ready, l * 8 + 8)
                            chain.link(nc.vector.scalar_tensor_tensor(s3[:, :], s3[:, :], 1.0, s1[:, :],
                                                                      ALU.add, ALU.mult))
                        if p == 11:
                            eng.wait_ge(decay_ready, l * 8 + 8)
                            eng.wait_ge(t_ready, l * 8 + 8)
                            chain.link(nc.vector.tensor_tensor(s1[:, :], s0[:, 0:2048], s0[:, 0:2048], ALU.mult))
                            nc.vector.scalar_tensor_tensor(s2[:, :], s1[:, :], 1.0, s2[:, :], ALU.add, ALU.mult
                                                           ).then_inc(v_ready, 1)
                        if p == 13:
                            eng.wait_ge(root_ready, l + 1)
                            chain.link(nc.vector.tensor_tensor(s3[:, :], s3[:, :], s2[:, :], ALU.mult))
                            for c in range(8):
                                nc.vector.tensor_tensor_scan(rec[:, c * S:(c + 1) * S], decay[:, c, :],
                                                             s3[:, c * S:(c + 1) * S], 0.0, ALU.mult, ALU.add
                                                             ).then_inc(rec_ready, 1)
                        if kind == "pl":
                            cols = slice((i - 17) * 1024, (i - 17) * 1024 + 1024)
                            eng.wait_ge(main.unit_used, done)
                            eng.wait_ge(pair_read[1], l * PAIR_READS[1] + 8)
                            eng.wait_ge(pair_read[0], l * PAIR_READS[0] + 8)
                            nc.vector.scalar_tensor_tensor(s2[:, cols], s2[:, cols], 1.0, pair[b][:, :],
                                                           ALU.add, ALU.mult).then_inc(pair_read[b], 1)
                        if 2 * ATT0 + 2 <= p <= 2 * ATT0 + 16 and p % 2 == 0:
                            h = (p - 2) // 2 - ATT0
                            eng.wait_ge(exp_ready, l * 16 + 2 * h + 2)
                            chain.link(nc.vector.reciprocal(rden[:, :], den[:, :]))
                            eng.wait_ge(pv_done, l * 8 + h + 1)
                            for t in range(NT):
                                nc.vector.tensor_scalar(attn[:, t, h * HD:(h + 1) * HD],
                                                        pO[:, t * HD:(t + 1) * HD], rden[:, t:t + 1], None,
                                                        ALU.mult).then_inc(attn_ready, 1)
                        if 2 * ATT0 <= p < 2 * (ATT0 + HEADS) and p % 2 == 0:
                            h = p // 2 - ATT0
                            eng.wait_ge(qk_done, l * 8 + h + 1)
                            if h:
                                eng.wait_ge(pT_done, l * 8 + h)
                            for t in (1, 0):
                                w = S if t else P
                                cols = slice(0, 768) if t else slice(768, 1152)
                                pr = probs[:, cols]
                                chain.link(nc.vector.scalar_tensor_tensor(
                                    pr.rearrange("p (g n) -> p g n", g=GROUPS),
                                    pS[:, cols].rearrange("p (g n) -> p g n", g=GROUPS), HD ** -0.5,
                                    mask[:, :, S - w:S], ALU.mult, ALU.add))
                            for t in range(NT):
                                pr = probs[:, 0:768] if t == 1 else probs[:, 768:1152]
                                nc.vector.tensor_reduce(nmax[:, t:t + 1], pr, AX.X, ALU.max, negate=True
                                                        ).then_inc(max_ready, 1)
                        if p in G_STEPS:
                            half = G_STEPS[p]
                            cols = slice(half * 1024, half * 1024 + 1024)
                            eng.wait_ge(g_ready, l * 2 + half + 1)
                            eng.wait_ge(pair_read[b], l * PAIR_READS[b] + (i // 2 + 1))
                            chain.link(nc.vector.tensor_scalar(s2[:, cols], s2[:, cols], 0.044715, 1.0,
                                                               ALU.mult, ALU.add))
                            nc.vector.tensor_tensor(s2[:, cols], s2[:, cols], s0[:, cols], ALU.mult
                                                    ).then_inc(g_inner, 1)
                        if p - 1 in G_STEPS:
                            half = G_STEPS[p - 1]
                            cols = slice(half * 1024, half * 1024 + 1024)
                            eng.wait_ge(g_tanh, l * 2 + half + 1)
                            eng.wait_ge(rec_ready, l * 8 + 8)
                            chain.link(nc.vector.scalar_tensor_tensor(s0[:, cols], s2[:, cols], 1.0, s0[:, cols],
                                                                      ALU.add, ALU.mult))
                            nc.vector.scalar_tensor_tensor(s2[:, cols], s0[:, cols], 0.5, rec[:, cols],
                                                           ALU.mult, ALU.mult).then_inc(lru_full, 1)
                        if p - 2 in G_STEPS:
                            half = G_STEPS[p - 2]
                            cols = slice(half * 1024, half * 1024 + 1024)
                            eng.wait_ge(lT_high, l * 2 + half + 1)
                            nc.vector.tensor_tensor(lru_l[:, cols], s2[:, cols], lru_h[:, cols].bitcast(f32),
                                                    ALU.subtract).then_inc(lT_low, 1)
                        if p == 38:
                            for n in range(2):
                                eng.wait_ge(aT_high, l * 2 + n + 1)
                                cols = slice(512 * n, 512 * n + 512)
                                nc.vector.tensor_tensor(att_l[:, cols], pS[:, cols], att_h[:, cols].bitcast(f32),
                                                        ALU.subtract).then_inc(aT_low, 1)
                        if kind == "pa":
                            half = i - 19
                            cols = slice(half * 1024, half * 1024 + 1024)
                            eng.wait_ge(main.unit_used, done)
                            eng.wait_ge(pair_read[0], l * PAIR_READS[0] + 9)
                            nc.vector.scalar_tensor_tensor(s0[:, cols], s0[:, cols], 1.0, pair[b][:, :],
                                                           ALU.add, ALU.mult).then_inc(pair_read[b], 1)
                            eng.wait_ge(pair_read[b], l * PAIR_READS[b] + (i // 2 + 1))
                            nc.vector.tensor_tensor(s0[:, cols], s0[:, cols], s2[:, cols], ALU.add
                                                    ).then_inc(mix_full, 1)
                            if half == 0:
                                split_w(l, p + 2)
                            eng.wait_ge(mix_high, l * 2 + half + 1)
                            nc.vector.scalar_tensor_tensor(act_l[:, cols], s0[:, cols], 0.5,
                                                           act_h[:, cols].bitcast(f32), ALU.mult, ALU.subtract
                                                           ).then_inc(mix_low, 1)
                            if half == 1:
                                split_w(l, p + 2)
                        if kind == "wo":
                            n = i - 21
                            eng.wait_ge(main.unit_used, done)
                            if n == 0:
                                nc.vector.tensor_tensor(xs[:, :, 0:512], xs[:, :, 0:512],
                                                        pair[b][:, :].rearrange("p (t n) -> p t n", t=NT), ALU.add
                                                        ).then_inc(x_mixed, 1)
                            else:
                                for t in range(NT):
                                    nc.vector.tensor_tensor(xs[:, t, 512:D], xs[:, t, 512:D],
                                                            pair[b][:, t * 512:(t + 1) * 512], ALU.add
                                                            ).then_inc(x_mixed, 1)
                        if p == W_UNITS - 2:
                            y_zeros(main)
                        if p == W_UNITS - 1:
                            split_w(l, W_UNITS + 1)
                eng.wait_ge(nrow_in, l * 16 + 16)
                for t in range(NT):
                    eng.wait_ge(rstd_ready, l * 4 + t + 3)
                    nc.vector.scalar_tensor_tensor(h2[:, t, :], xs[:, t, :], rstd[:, t:t + 1], nrow,
                                                   ALU.mult, ALU.mult).then_inc(h2_ready, 1)
                eng.wait_ge(logits_done, l + 1)
                for t in range(NT):
                    ps = logits[t]
                    chain.step(nc.vector.scalar_tensor_tensor(lg[:, t, :], ps, rstd[:, t:t + 1],
                                                              cur[:, C_RB:C_RB + 20], ALU.mult, ALU.add))
                    chain.step(nc.vector.scalar_tensor_tensor(g8[:, t, 0:EG], ps[:, 0:EG], rstd[:, t:t + 1],
                                                              cur[:, C_RB:C_RB + EG], ALU.mult, ALU.add))

                def top8(values, top, index):
                    chain.join()
                    settled(eng)
                    for t in range(NT):
                        chain.step(nc.vector.max(top[:, t, :], values[:, t, :]))
                    chain.join()
                    settled(eng)
                    for t in range(NT):
                        chain.step(nc.vector.max_index(index[:, t, :], top[:, t, :], values[:, t, :]))

                top8(g8, gm, gi)
                nc.vector.tensor_scalar(rs[:, 0, :], gm[:, :, 0:1].rearrange("p t o -> p (t o)"), -1.0, None,
                                        ALU.mult).then_inc(gneg_ready, 1)
                chain.join()
                chain.link(nc.vector.tensor_copy(gf[:, :, 0:1], gi[:, :, 0:1]))
                chain.link(nc.vector.tensor_tensor(goh[:, :, :], iota[:, 0:EG].unsqueeze(1).to_broadcast([P, NT, EG]),
                                                   gf[:, :, 0:1].to_broadcast([P, NT, EG]), ALU.is_equal))
                goh4 = goh[:, :, :].unsqueeze(3).to_broadcast([P, NT, EG, EG])
                chain.link(nc.vector.tensor_tensor(
                    r16[:, :, :].rearrange("p t (g j) -> p t g j", g=EG),
                    lg[:, :, EG:20].rearrange("p t (g j) -> p t g j", g=EG), goh4, ALU.mult))
                chain.step(nc.vector.tensor_reduce(
                    e8[:, :, 0:EG], r16[:, :, :].rearrange("p t (g j) -> p t j g", g=EG), AX.X, ALU.add))
                top8(e8, em, ei)
                nc.vector.tensor_tensor(rs[:, 2, :], em[:, :, 1:2].rearrange("p t o -> p (t o)"),
                                        em[:, :, 0:1].rearrange("p t o -> p (t o)"), ALU.subtract
                                        ).then_inc(diff_ready, 1)
                chain.join()
                chain.link(nc.vector.tensor_copy(ef[:, :, 0:2], ei[:, :, 0:2]))
                for n in range(2):
                    chain.step(nc.vector.tensor_tensor(
                        oh[:, n, :, :], iota[:, 0:EG].unsqueeze(1).to_broadcast([P, NT, EG]),
                        ef[:, :, n:n + 1].to_broadcast([P, NT, EG]), ALU.is_equal))
                chain.join()
                chain.link(nc.vector.tensor_tensor(oh_sum[:, :, :], oh[:, 0, :, :], oh[:, 1, :, :], ALU.add))
                nc.vector.tensor_tensor(sel[:, :, :].rearrange("p t (g j) -> p t g j", g=EG), goh4,
                                        oh_sum[:, :, :].unsqueeze(2).to_broadcast([P, NT, EG, EG]), ALU.mult
                                        ).then_inc(sel_ready, 1)
                eng.wait_ge(rank_done, l + 1)
                eng.wait_ge(sel_ready, l + 1)
                chain.link(nc.vector.scalar_tensor_tensor(
                    rank[:, :, 0:NE], pO[:, 64:96].rearrange("p (t n) -> p t n", t=NT), 1.0,
                    sel[:, :, :].bitcast(f32), ALU.add, ALU.mult))
                chain.link(nc.vector.tensor_scalar(rank[:, :, 0:NE], rank[:, :, 0:NE], -1.0, None, ALU.add))
                slots_of(main, 0)
                chain.link(nc.vector.tensor_reduce(over[:, :], pO[:, 128:128 + NE], AX.X, ALU.max))
                nc.vector.tensor_scalar(flag[:, :], over[:, :], float(CAP) + 0.5, None, ALU.is_ge
                                        ).then_inc(flag_ready, 1)
                eng.wait_ge(e2_ready, l + 1)
                eng.wait_ge(gexp_ready, l * 2 + 2)
                chain.link(nc.vector.scalar_tensor_tensor(rs[:, 4, :], rs[:, 3, :], 1.0, rs[:, 1, :], ALU.add,
                                                          ALU.mult))
                chain.link(nc.vector.reciprocal(rs[:, 4, :], rs[:, 4, :]))
                chain.link(nc.vector.tensor_tensor(rs[:, 5, :], rs[:, 4, :], rs[:, 3, :], ALU.mult))
                for n in range(2):
                    chain.step(nc.vector.tensor_tensor(
                        oh[:, n, :, :], oh[:, n, :, :],
                        rs[:, 4 + n, :].unsqueeze(2).to_broadcast([P, NT, EG]), ALU.mult))
                chain.join()
                chain.link(nc.vector.tensor_tensor(oh_sum[:, :, :], oh[:, 0, :, :], oh[:, 1, :, :], ALU.add))
                nc.vector.tensor_tensor(comb[:, :, :].rearrange("p t (g j) -> p t g j", g=EG), goh4,
                                        oh_sum[:, :, :].unsqueeze(2).to_broadcast([P, NT, EG, EG]), ALU.mult
                                        ).then_inc(comb_ready, 1)
                assert chain.n == DVE_LINKS, f"DVE_LINKS = {chain.n}"
                moe(main, l, W_UNITS)
                eng.wait_ge(flag_ready, l + 1)
                settled(eng)
                more = eng.value_load(flag[0:1, 0:1], min_val=0, max_val=1)
                with eng.If(more > 0):
                    add_experts(main, l, main.x_added)
                    eng.wait_ge(main.x_added, l * 2 + 2)
                    settled(eng)
                    with eng.Fori(0, MORE) as q:
                        n = l * MORE + q
                        nc.vector.tensor_scalar(rank[:, :, :], rank[:, :, :], -float(CAP), None, ALU.add
                                                ).then_inc(rank_moved, 1)
                        for j in range(2):
                            split_low(over_flow, n * M_UNITS + j + 1, j, j)
                        y_zeros(over_flow)
                        eng.wait_ge(rank_moved, n + 1)
                        slots_of(over_flow, 0)
                        moe(over_flow, n, 0)
                        add_experts(over_flow, n, over_flow.x_added)
                        eng.wait_ge(over_flow.x_added, n * 2 + 2)
                    eng.sem_inc(x_done, NT)
                with eng.Else():
                    eng.sem_inc(rank_moved, MORE)
                    for sm, k in ((over_flow.low_dve, M_UNITS), (over_flow.p_ready, NE + 1),
                                  (over_flow.ws_ready, NE), (over_flow.he_low0, NE + 1),
                                  (over_flow.he_low1, NE + 1), (over_flow.act_ready, NE), (over_flow.ae_low, NE),
                                  (over_flow.g_sum, NE),
                                  (over_flow.y_low0, NE), (over_flow.y_low1, NE), (over_flow.y_zero, 1),
                                  (over_flow.x_added, 2), (over_flow.dve_chain, NE)):
                        eng.sem_inc(sm, k * MORE)
                    add_experts(main, l, x_done)
                    eng.sem_inc(main.x_added, NT)
            eng.wait_ge(nrow_in, 16 * (LAYERS + 1))
            for t in range(NT):
                eng.wait_ge(rstd_ready, LAYERS * 4 + t + 1)
                nc.vector.scalar_tensor_tensor(xn[:, t, :], xs[:, t, :], rstd[:, t:t + 1], nrow, ALU.mult,
                                               ALU.mult).then_inc(out_done, 1)

        @block.tensor
        def _(pe_eng):
            eng = pe_eng
            mm = nc.tensor.matmul
            for flow in (main, over_flow):
                eng.sem_inc(flow.unit_used, SLOTS)

            def unit_there(flow, count):
                eng.wait_ge(flow.low_dve, count + CREDIT)
                eng.wait_ge(flow.low_pool, count + CREDIT)

            def tok_unit(slot, xh, xl, outs, k0, start, stop):
                for t in range(len(outs)):
                    for k in range(4):
                        w = slice(k * 512, (k + 1) * 512)
                        mm(outs[t], xh(k0 + k, t), high[:, slot, w], start=start and k == 0, stop=False)
                        mm(outs[t], xh(k0 + k, t), low[:, slot, w], start=False, stop=False)
                        ins = mm(outs[t], xl(k0 + k, t), high[:, slot, w], start=False, stop=stop and k == 3)
                return ins

            def feat_unit(slot, xh, xl, out, ktiles, first_of=None):
                width = UCOL // ktiles
                for f in range(width // P):
                    o = out[:, f * S:(f + 1) * S]
                    for k in range(ktiles):
                        if first_of is not None and f == 0 and k % 2 == 0:
                            eng.wait_ge(hT_low, first_of * 8 + k + 2)
                        w = slice(k * width + f * P, k * width + (f + 1) * P)
                        mm(o, high[:, slot, w], xh[:, k, :], start=k == 0, stop=False)
                        mm(o, high[:, slot, w], xl[:, k, :], start=False, stop=False)
                        ins = mm(o, low[:, slot, w], xh[:, k, :], start=False, stop=k == ktiles - 1)
                return ins

            def scatter(flow, l, e, halves, stop):
                for half in halves:
                    eng.wait_ge([flow.y_low0, flow.y_low1][half], l * NE + e + 1)
                for t in range(NT):
                    for half in halves:
                        cols = slice(512 * half, 512 * half + 512)
                        mm(pair[t][:, cols], pt_01[:, t * P:(t + 1) * P], y_h[:, cols], start=False, stop=False)
                        ins = mm(pair[t][:, cols], pt_01[:, t * P:(t + 1) * P], y_l[:, cols], start=False,
                                 stop=stop)
                    if stop:
                        ins.then_inc(flow.moe_done, 1)

            def gather(flow, l, e_next, half):
                for c in range(4 * half, 4 * half + 4):
                    n = 0
                    for t in range(NT):
                        for part in (h2_h, h2_l):
                            ins = mm(bank[2 + half][:, (c % 4) * P:(c % 4 + 1) * P],
                                     part[:, t, c * P:(c + 1) * P], pe_01[:, t, :], start=n == 0,
                                     stop=n == 3)
                            n += 1
                ins.then_inc([flow.he_done0, flow.he_done1][half], 1)

            def zero_sums(flow, l):
                eng.wait_ge(flow.y_zero, l + 1)
                for t in range(NT):
                    for half in range(2):
                        mm(pair[t][:, 512 * half:512 * half + 512], pt_01[:, 0:P], y_h[:, 0:512], start=True,
                           stop=False)

            def gather_first(flow, n, l):
                eng.wait_ge(flow.p_ready, n * (NE + 1) + 1)
                gather(flow, n, 0, 0)
                eng.wait_ge(flag_ready, l + 1)
                gather(flow, n, 0, 1)

            def transpose_x(l, half, count, out):
                for t in range(NT):
                    eng.wait_ge(x_mixed, count + (t if half else 0))
                    for c in range(4):
                        ins = nc.tensor.transpose(out[:, c * S + t * P:c * S + (t + 1) * P],
                                                  xs[:, t, (4 * half + c) * P:(4 * half + c + 1) * P],
                                                  ident[:, :])
                        if t == NT - 1 and c % 2:
                            ins.then_inc(x2T_done, 1)

            def moe(flow, l, first):
                def unit(e, j, x, out, k0, start, stop):
                    slot = (first + j) % SLOTS
                    unit_there(flow, l * flow.units + e * E_UNITS + (first + j + 1))
                    for k in range(4):
                        w = slice(k * 512, (k + 1) * 512)
                        mm(out, x[:, k0 + k, :], high[:, slot, w], start=start and k == 0, stop=False)
                        ins = mm(out, x[:, k0 + k, :], low[:, slot, w], start=False, stop=stop and k == 3)
                    ins.then_inc(flow.unit_used, 1)

                with eng.Fori(0, NE) as e:
                    for half in range(2):
                        eng.wait_ge([flow.he_low0, flow.he_low1][half], l * (NE + 1) + e + 1)
                        unit(e, half, he, bank[0], 4 * half, half == 0, half == 1)
                        scatter(flow, l, e, (half,), False)
                    for t in range(NT):
                        nc.tensor.transpose(bank[2][:, t * P:(t + 1) * P], pe_01[:, t, :].bitcast(f32),
                                            ident[:, :])
                    for t in range(NT):
                        ins = mm(bank[2][:, S:S + 1], pe_01[:, t, :].bitcast(f32), comb[:, t, ds(e, 1)],
                                 start=t == 0, stop=t == NT - 1)
                    ins.then_inc(flow.pt_done, 1)
                    for half in range(2):
                        unit(e, 2 + half, he, bank[1], 4 * half, half == 0, half == 1)
                    eng.wait_ge(flow.p_ready, l * (NE + 1) + e + 2)
                    eng.wait_ge(flow.ws_ready, l * NE + e + 1)
                    gather(flow, l, e + 1, 0)
                    eng.wait_ge(flow.act_ready, l * NE + e + 1)
                    settled(eng)
                    for c in range(4):
                        ins = mm(bank[0][:, c * CAP:(c + 1) * CAP], act[:, c * P:(c + 1) * P], ident2[:, :],
                                 start=True, stop=True)
                    ins.then_inc(flow.aeT_done, 1)
                    gather(flow, l, e + 1, 1)
                    eng.wait_ge(flow.ae_low, l * NE + e + 1)
                    for half in range(2):
                        if half:
                            eng.wait_ge(flow.he_low0, l * (NE + 1) + e + 2)
                        unit(e, 4 + half, ae, bank[1 + half], 0, True, True)
                scatter(flow, l, NE, (0, 1), True)

            eng.wait_ge(const_in, 112)
            eng.wait_ge(table_zero, 7)
            with eng.Fori(0, LAYERS) as l:
                for t in range(NT):
                    eng.wait_ge(xn_ready, l * 2 + t + 1)
                    for c in range(8):
                        col = (c % 4) * S + t * P
                        ins = nc.tensor.transpose(pair[c // 4][:, col:col + P], xn[:, t, c * P:(c + 1) * P],
                                                  ident[:, :])
                        if t == NT - 1 and c % 2:
                            ins.then_inc(xT_done, 1)
                for i in range(NG):
                    kind, b = GROUP_KINDS[i], i % 2
                    outs = [pair[b][:, 0:512], pair[b][:, 512:1024]]
                    head = i - ATT0
                    if i >= 2:
                        eng.wait_ge(pair_read[b], l * PAIR_READS[b] + i // 2)
                    if 0 <= head < HEADS:
                        if head == 0:
                            eng.wait_ge(qkT_ready, l * 12 + 12)
                            eng.wait_ge(r_ready, l * 8 + 8)
                            eng.wait_ge(i_ready, l * 8 + 8)
                        else:
                            eng.wait_ge(pT_ready, l * 8 + head)
                        hp = slice((head % 2) * HD, (head % 2) * HD + HD)
                        for g in range(GROUPS):
                            c = 4 * g + head // 2
                            mm(pS[:, g * S:(g + 1) * S], qT[hp, c, P:S], kT[hp, c, :], start=True, stop=True)
                        for g in range(GROUPS):
                            c = 4 * g + head // 2
                            ins = mm(pS[:, 768 + g * P:768 + (g + 1) * P], qT[hp, c, 0:P], kT[hp, c, 0:P],
                                     start=True, stop=True)
                        ins.then_inc(qk_done, 1)
                    for n in range(GROUP_UNITS[i]):
                        u = GROUP_START[i] + n
                        unit_there(main, l * UNITS + u + 1)
                        last = n == GROUP_UNITS[i] - 1
                        if kind in ("u", "g", "m"):
                            ins = feat_unit(u % SLOTS, hT_h, hT_l, outs[n], KD, l if u == 0 else None)
                        elif kind in ("q", "k", "v"):
                            ins = tok_unit(u % SLOTS, lambda k, t: hT_h[:, k, t * P:(t + 1) * P],
                                           lambda k, t: hT_l[:, k, t * P:(t + 1) * P], outs, 4 * n, n == 0, last)
                        elif kind == "pl":
                            if n == 0:
                                eng.wait_ge(lT_low, l * 2 + 2)
                            ins = feat_unit(u % SLOTS, lT_h, lT_l, outs[n], KD)
                        elif kind == "pa":
                            eng.wait_ge(aT_low, l * 2 + 2)
                            ins = feat_unit(u % SLOTS, aT_h, aT_l, pair[b], 4)
                        else:
                            eng.wait_ge(mix_low, l * 2 + n + 1)
                            ins = tok_unit(u % SLOTS, lambda k, t: hT_h[:, k, t * P:(t + 1) * P],
                                           lambda k, t: hT_l[:, k, t * P:(t + 1) * P], outs, 4 * n, n == 0, last)
                        ins.then_inc(main.unit_used, 1)
                        p = u + 1
                        if p == W_UNITS - 1:
                            transpose_x(l, 0, l * 3 + 1, pair[1])
                        if 5 <= p <= 8:
                            for c in range(2 * (p - 5), 2 * (p - 5) + 2):
                                if c == 0:
                                    eng.wait_ge(bd_in, l * 16 + 16)
                                eng.wait_ge(conv_ready, l * 8 + c + 1)
                                if c >= 3:
                                    eng.wait_ge(r_ready, l * 8 + c - 2)
                                    eng.wait_ge(i_ready, l * 8 + c - 2)
                                mm(pS[:, (c % 3) * 512:(c % 3) * 512 + S], bd[:, 0, c, :], conv[:, c, :],
                                   start=True, stop=True)
                                mm(pS[:, (c % 3) * 512 + S:(c % 3) * 512 + 2 * S], bd[:, 1, c, :], conv[:, c, :],
                                   start=True, stop=True).then_inc(gate_mm, 1)
                        for tile in range(NT):
                            j = GROUP_END.get(p - 1 - tile)
                            if j is not None and GROUP_KINDS[j] in "qk":
                                m = (j - 2) * NT + tile
                                eng.wait_ge(rot_ready, l * 12 + m + 1)
                                if m:
                                    eng.wait_ge(qkT_ready, l * 12 + m)
                                for c in range(4):
                                    ins = nc.tensor.transpose(
                                        pO[:, c * P:(c + 1) * P],
                                        v[:, 0, 512 + 512 * tile + c * P:512 + 512 * tile + (c + 1) * P],
                                        ident[:, :])
                                ins.then_inc(rotT_done, 1)
                        if 0 <= head < HEADS and n == 0:
                            eng.wait_ge(exp_ready, l * 16 + 2 * head + 2)
                            for blk in range(9):
                                ins = nc.tensor.transpose(pS[:, blk * P:(blk + 1) * P],
                                                          probs[:, blk * P:(blk + 1) * P], ident[:, :])
                            ins.then_inc(pT_done, 1)
                        if 0 <= head < HEADS and n == 1:
                            eng.wait_ge(pT_ready, l * 8 + head + 1)
                            if head == 0:
                                eng.wait_ge(pair_read[0], l * PAIR_READS[0] + 6)
                                eng.wait_ge(pair_read[1], l * PAIR_READS[1] + 5)
                            else:
                                eng.wait_ge(attn_ready, l * 16 + 2 * head)
                            for blk in range(6):
                                g, kb = blk // 2, blk % 2
                                mm(pO[:, HD:2 * HD], pT[:, blk * P:(blk + 1) * P],
                                   v[:, kb, g * 512 + head * HD:g * 512 + (head + 1) * HD],
                                   start=blk == 0, stop=blk == 5)
                            for g in range(GROUPS):
                                ins = mm(pO[:, 0:HD], pT[:, 768 + g * P:768 + (g + 1) * P],
                                         v[:, 0, g * 512 + head * HD:g * 512 + (head + 1) * HD],
                                         start=g == 0, stop=g == GROUPS - 1)
                            ins.then_inc(pv_done, 1)
                        if p == 38:
                            eng.wait_ge(attn_ready, l * 16 + 16)
                            for c in range(4):
                                for t in range(NT):
                                    ins = nc.tensor.transpose(pS[:, c * S + t * P:c * S + (t + 1) * P],
                                                              attn[:, t, c * P:(c + 1) * P], ident[:, :])
                                if c % 2:
                                    ins.then_inc(aT_done, 1)
                eng.wait_ge(rw_ready, l + 1)
                for half in range(2):
                    if half:
                        transpose_x(l, 1, l * 3 + 2, pS)
                    eng.wait_ge(x2T_ready, l * 4 + 2 * half + 2)
                    for t in range(NT):
                        for k in range(4 * half, 4 * half + 4):
                            ins = mm(logits[t], x2T[:, k, t * P:(t + 1) * P],
                                     cur[:, C_RW + 20 * k:C_RW + 20 * (k + 1)], start=k == 0, stop=k == KD - 1)
                ins.then_inc(logits_done, 1)
                zero_sums(main, l)
                eng.wait_ge(sel_ready, l + 1)
                mm(pO[:, 64:80], tri[:, :], sel[:, 0, :], start=True, stop=True)
                mm(pO[:, 80:96], ones[:, :], sel[:, 0, :], start=True, stop=False)
                mm(pO[:, 80:96], tri[:, :], sel[:, 1, :], start=False, stop=True)
                mm(pO[:, 128:144], ones[:, :], sel[:, 0, :], start=True, stop=False)
                mm(pO[:, 128:144], ones[:, :], sel[:, 1, :], start=False, stop=True).then_inc(rank_done, 1)
                eng.wait_ge(h2_low, l * 2 + 2)
                gather_first(main, l, l)
                eng.wait_ge(comb_ready, l + 1)
                settled(eng)
                moe(main, l, W_UNITS)
                eng.wait_ge(flag_ready, l + 1)
                settled(eng)
                more = eng.value_load(flag[0:1, 0:1], min_val=0, max_val=1)
                with eng.If(more > 0):
                    eng.wait_ge(main.x_added, l * 2 + 2)
                    settled(eng)
                    with eng.Fori(0, MORE) as q:
                        n = l * MORE + q
                        zero_sums(over_flow, n)
                        gather_first(over_flow, n, l)
                        moe(over_flow, n, 0)
                        eng.wait_ge(over_flow.x_added, n * 2 + 2)
                        settled(eng)
                with eng.Else():
                    for sm, k in ((over_flow.unit_used, M_UNITS), (over_flow.pt_done, NE),
                                  (over_flow.he_done0, NE + 1), (over_flow.he_done1, NE + 1),
                                  (over_flow.aeT_done, NE), (over_flow.moe_done, NT)):
                        eng.sem_inc(sm, k * MORE)


def kernel(**inputs):
    import concourse.bacc as bacc
    from concourse.bass_utils import run_bass_kernel_spmd as run

    def arr(name):
        return np.ascontiguousarray(inputs[name])

    w_in, wpa, wpl, wo = arr("w_in"), arr("w_proj_attn"), arr("w_proj_lru"), arr("w_out")
    wg, wu, wd = arr("expert_w_gate"), arr("expert_w_up"), arr("expert_w_down")
    stream = np.empty((LAYERS * UNITS, P, UCOL), np.float32)

    def k_units(row, w):
        stream[row:row + 2] = w.reshape(2, 4, P, 512).transpose(0, 2, 1, 3).reshape(2, P, UCOL)

    def f_units(row, w):
        stream[row:row + 2] = w.reshape(KD, P, 2, 256).transpose(2, 1, 0, 3).reshape(2, P, UCOL)

    def n_units(row, w):
        stream[row:row + 2] = w.reshape(4, P, 2, 512).transpose(2, 1, 0, 3).reshape(2, P, UCOL)

    A = 1536
    u0, g0, m0 = 3 * A, 3 * A + D, 3 * A + 2 * D
    cols = ([u0, u0 + 512] + [n * 512 for n in range(9)] + [g0, g0 + 512]
            + [m0 + D, m0 + D + 512, m0, m0 + 512])
    for l in range(LAYERS):
        row = l * UNITS
        for kind, c in zip(GROUP_KINDS, cols):
            (k_units if kind in "qkv" else f_units)(row, w_in[l][:, c:c + 512])
            row += 2
        for n in range(2):
            f_units(row, wpl[l][:, n * 512:(n + 1) * 512])
            row += 2
        n_units(row, wpa[l])
        row += 2
        for n in range(2):
            k_units(row, wo[l][:, n * 512:(n + 1) * 512])
            row += 2
        for e in range(NE):
            k_units(row, wg[l, e])
            k_units(row + 2, wu[l, e])
            n_units(row + 4, wd[l, e])
            row += 6

    small = np.zeros((P, LAYERS, SMALL), np.float32)

    def put(col, a):
        a = a.reshape(LAYERS, -1, P)
        small[:, :, col:col + a.shape[1]] = a.transpose(2, 0, 1)

    for col, name in ((C_N1, "norm1_scale"), (C_N2, "norm2_scale"), (C_BA, "lru_ba"), (C_BX, "lru_bx"),
                      (C_LAM, "lru_lambda"),
                      (C_CB, "conv_b"), (C_CW, "conv_w"), (C_BM, "b_merge")):
        put(col, arr(name))
    rw = np.concatenate([arr("router_group_w"), arr("router_expert_w")], axis=2)
    small[:, :, C_RW:C_RW + 160] = rw.reshape(LAYERS, KD, P, 20).transpose(2, 0, 1, 3).reshape(P, LAYERS, 160)
    small[:, :, C_RB:C_RB + EG] = arr("router_group_b")[None]
    small[:, :, C_RB + EG:C_RB + 20] = arr("router_expert_b")[None]

    blockdiag = np.zeros((LAYERS, P, 2, 8, P), np.float32)
    for n, name in enumerate(("lru_wa", "lru_wx")):
        w = arr(name).reshape(LAYERS, 8, 2, HD, HD)
        for b in range(2):
            blockdiag[:, b * HD:(b + 1) * HD, n, :, b * HD:(b + 1) * HD] = w[:, :, b].transpose(0, 2, 1, 3)

    norm_rows = np.empty((LAYERS + 1, P, D), np.float32)
    norm_rows[:LAYERS] = arr("norm2_scale")[:, None, :]
    norm_rows[LAYERS] = arr("final_norm_scale")[None, :]

    tables = np.zeros((P, 768), np.float32)
    tables[:, 0:128] = np.eye(P, dtype=np.float32)
    tables[:, 384:384 + CAP] = np.tile(np.eye(CAP, dtype=np.float32), (2, 1))
    tables[:, 128:256] = np.triu(np.ones((P, P), np.float32), 1)
    tables[:, 256:384] = np.tile(np.arange(CAP, dtype=np.float32), 2)[None]
    inv = (10000.0 ** (-np.arange(0, HD, 2, dtype=np.float32) / np.float32(HD))).astype(np.float32)
    ang = (np.arange(S, dtype=np.float32)[:, None] * inv[None, :]).astype(np.float32)
    cos, sin = np.cos(ang).astype(np.float32), np.sin(ang).astype(np.float32)
    tables[:, 512:640] = np.concatenate([cos, cos], 1).reshape(NT, P, HD).transpose(1, 0, 2).reshape(P, 128)
    tables[:, 640:768] = np.concatenate([-sin, sin], 1).reshape(NT, P, HD).transpose(1, 0, 2).reshape(P, 128)
    dist = (P + np.arange(P))[:, None] - np.arange(S)[None, :]
    masks = np.zeros((P, GROUPS, S), np.float32)
    for g, (window, dilation) in enumerate(WINDOWS):
        ok = (dist >= 0) & (dist <= window) & (dist % dilation == 0)
        masks[:, g, :] = np.where(ok, 0.0, NEG)

    feeds = {
        "stream": stream,
        "x_in": np.ascontiguousarray(arr("x").reshape(NT, P, D).transpose(1, 0, 2)),
        "small": small,
        "blockdiag": blockdiag.reshape(LAYERS, P, 2048),
        "norm_rows": norm_rows,
        "tables": tables,
        "masks": masks.reshape(P, GROUPS * S),
    }
    nc = bacc.Bacc("TRN2", target_bir_lowering=False, num_devices=1)
    aps = [nc.dram_tensor(n, a.shape, mybir.dt.float32, kind="ExternalInput").ap() for n, a in feeds.items()]
    o = nc.dram_tensor("out", (P, NT, D), mybir.dt.float32, kind="ExternalOutput").ap()
    build(nc, *aps, o)
    r = run(nc, [feeds], core_ids=[0])
    return np.ascontiguousarray(r.results[0]["out"].transpose(1, 0, 2)).reshape(1, S, D)
```
